# Optimizing a Trainium2 kernel written in Bass

```python
import math
import jax, jax.numpy as jnp
from jax import lax
import numpy as np

D_MODEL = 1024
BATCH = 1
SEQ = 256
DEPTH = 1

CHUNK = 64
Q_BLOCK = 128
EPS = 1e-6
ROPE_THETA = 10000.0
DIFF_HEADS = 4
DIFF_HEAD_DIM = 64
DIFF_V_DIM = 2 * DIFF_HEAD_DIM
DIFF_WIDTH = DIFF_HEADS * 2 * DIFF_HEAD_DIM
CONV_WIDTH = 512
CONV_K = 3
N_MEM = 256
MEM_HEADS = 4
MEM_HEAD_DIM = 128
MEM_WIDTH = MEM_HEADS * MEM_HEAD_DIM
N_BRANCH = 3
BRANCH_WIDTH = 512
IN_SIZES = (DIFF_WIDTH, DIFF_WIDTH, DIFF_WIDTH,
            CONV_WIDTH, CONV_WIDTH, CONV_WIDTH,
            MEM_WIDTH, N_BRANCH * D_MODEL)
IN_TOTAL = sum(IN_SIZES)
N_EXPERTS = 32
TOP_K = 4
D_FF = D_MODEL
SWIGLU_LIMIT = 7.0
SWIGLU_ALPHA = 1.702
MOE_BLOCK = 256

kernel_name = "hybrid_diffattn_shortconv_memxattn_moe"

def rmsnorm(x, g):
    xf = x.astype(jnp.float32)
    y = xf * lax.rsqrt(jnp.mean(xf * xf, axis=-1, keepdims=True) + EPS)
    return (y * g.astype(jnp.float32)).astype(x.dtype)

def rope(x, cos, sin):
    x1, x2 = jnp.split(x, 2, axis=-1)
    return jnp.concatenate([x1 * cos - x2 * sin, x2 * cos + x1 * sin], axis=-1)

def diff_attention(q, k, v, lam):
    B, S = q.shape[0], q.shape[1]
    n_qb = S // Q_BLOCK
    qb = q.reshape(B, n_qb, Q_BLOCK, DIFF_HEADS, 2, DIFF_HEAD_DIM).swapaxes(0, 1)
    key_chunk = jnp.arange(S) // CHUNK
    scale = DIFF_HEAD_DIM ** -0.5

    def block(args):
        q_blk, bi = args
        q_chunk = (bi * Q_BLOCK + jnp.arange(Q_BLOCK)) // CHUNK
        allowed = key_chunk[None, :] <= q_chunk[:, None]
        s = jnp.einsum('bqhcd,bkhcd->bhcqk', q_blk, k).astype(jnp.float32) * scale
        p = jax.nn.softmax(jnp.where(allowed, s, -jnp.inf), axis=-1)
        a = p[:, :, 0] - lam * p[:, :, 1]
        return jnp.einsum('bhqk,bkhe->bqhe', a.astype(v.dtype), v)

    out = lax.map(block, (qb, jnp.arange(n_qb)))
    return out.swapaxes(0, 1).reshape(B, S, DIFF_HEADS, DIFF_V_DIM)

def causal_depthwise_conv(u, w):
    return lax.conv_general_dilated(
        u, w[:, None, :].astype(u.dtype), window_strides=(1,),
        padding=[(CONV_K - 1, 0)], dimension_numbers=('NWC', 'WIO', 'NWC'),
        feature_group_count=u.shape[-1])

def memory_cross_attention(q, mem, g_mem, w_mem_kv, g_q, g_k):
    B, S = q.shape[0], q.shape[1]
    kv = rmsnorm(mem, g_mem) @ w_mem_kv
    k, v = jnp.split(kv, 2, axis=-1)
    M = mem.shape[1]
    k = rmsnorm(k.reshape(B, M, MEM_HEADS, MEM_HEAD_DIM), g_k)
    v = v.reshape(B, M, MEM_HEADS, MEM_HEAD_DIM)
    q = rmsnorm(q.reshape(B, S, MEM_HEADS, MEM_HEAD_DIM), g_q)
    s = jnp.einsum('bshd,bmhd->bhsm', q, k).astype(jnp.float32) * (MEM_HEAD_DIM ** -0.5)
    p = jax.nn.softmax(s, axis=-1)
    o = jnp.einsum('bhsm,bmhd->bshd', p.astype(v.dtype), v)
    return o.reshape(B, S, MEM_WIDTH)

def moe(h, w_router, b_router, w_gate_up, b_gate_up, w_down, b_down):
    B, S, D = h.shape
    T = B * S
    xt = h.reshape(T, D)
    logits = (xt @ w_router).astype(jnp.float32) + b_router.astype(jnp.float32)
    top_vals, top_idx = lax.top_k(logits, TOP_K)
    gates = jax.nn.softmax(top_vals, axis=-1)
    n_assign = T * TOP_K
    expert_flat = top_idx.reshape(-1)
    token_flat = jnp.arange(n_assign, dtype=jnp.int32) // TOP_K
    gate_flat = gates.reshape(-1)
    order = jnp.argsort(expert_flat)
    sorted_expert = expert_flat[order]
    counts = jnp.bincount(expert_flat, length=N_EXPERTS)
    padded = (counts + MOE_BLOCK - 1) // MOE_BLOCK * MOE_BLOCK
    start = jnp.cumsum(counts) - counts
    pend = jnp.cumsum(padded)
    pstart = pend - padded
    dest = pstart[sorted_expert] + (jnp.arange(n_assign) - start[sorted_expert])
    n_rows = -(-(n_assign + N_EXPERTS * (MOE_BLOCK - 1)) // MOE_BLOCK) * MOE_BLOCK
    n_blocks = n_rows // MOE_BLOCK
    row_token = jnp.zeros((n_rows,), jnp.int32).at[dest].set(token_flat[order])
    row_gate = jnp.zeros((n_rows,), jnp.float32).at[dest].set(gate_flat[order])
    block_expert = jnp.minimum(
        jnp.searchsorted(pend, jnp.arange(n_blocks) * MOE_BLOCK, side='right'),
        N_EXPERTS - 1)
    xs = xt[row_token].reshape(n_blocks, MOE_BLOCK, D)

    def expert_block(args):
        xb, e = args
        gu = xb @ w_gate_up[e] + b_gate_up[e]
        g, u = jnp.split(gu, 2, axis=-1)
        g = jnp.minimum(g, SWIGLU_LIMIT)
        u = jnp.clip(u, -SWIGLU_LIMIT, SWIGLU_LIMIT)
        act = (u + 1.0) * (g * jax.nn.sigmoid(g * SWIGLU_ALPHA))
        return act @ w_down[e] + b_down[e]

    ys = lax.map(expert_block, (xs, block_expert)).reshape(n_rows, D)
    ys = ys * row_gate[:, None].astype(ys.dtype)
    out = jax.ops.segment_sum(ys, row_token, num_segments=T)
    return out.reshape(B, S, D)

def setup_inputs(seed: int = 0) -> dict:
    key = jax.random.key(seed)
    ks = jax.random.split(key, 26)
    f32 = jnp.float32
    L, D, E = DEPTH, D_MODEL, N_EXPERTS

    def nrm(k, shape, scale):
        return jax.random.normal(k, shape, f32) * scale

    def gain(k, shape):
        return 1.0 + 0.02 * jax.random.normal(k, shape, f32)

    return {
        "x": nrm(ks[0], (BATCH, SEQ, D), 1.0),
        "mem": nrm(ks[1], (BATCH, N_MEM, D), 1.0),
        "g_mix": gain(ks[2], (L, D)),
        "w_in": nrm(ks[3], (L, D, IN_TOTAL), D ** -0.5),
        "g_q_diff": gain(ks[4], (L, DIFF_HEAD_DIM)),
        "g_k_diff": gain(ks[5], (L, DIFF_HEAD_DIM)),
        "lambda_q1": nrm(ks[6], (L, DIFF_HEAD_DIM), 0.1),
        "lambda_k1": nrm(ks[7], (L, DIFF_HEAD_DIM), 0.1),
        "lambda_q2": nrm(ks[8], (L, DIFF_HEAD_DIM), 0.1),
        "lambda_k2": nrm(ks[9], (L, DIFF_HEAD_DIM), 0.1),
        "g_subln": gain(ks[10], (L, DIFF_V_DIM)),
        "conv_w": nrm(ks[11], (L, CONV_K, CONV_WIDTH), CONV_K ** -0.5),
        "g_mem": gain(ks[12], (L, D)),
        "w_mem_kv": nrm(ks[13], (L, D, 2 * MEM_WIDTH), D ** -0.5),
        "g_q_mem": gain(ks[14], (L, MEM_HEAD_DIM)),
        "g_k_mem": gain(ks[15], (L, MEM_HEAD_DIM)),
        "w_branch": nrm(ks[16], (L, N_BRANCH, BRANCH_WIDTH, D), BRANCH_WIDTH ** -0.5),
        "w_out": nrm(ks[17], (L, D, D), D ** -0.5),
        "g_ffn": gain(ks[18], (L, D)),
        "w_router": nrm(ks[19], (L, D, E), D ** -0.5),
        "b_router": nrm(ks[20], (L, E), 0.01),
        "w_gate_up": nrm(ks[21], (L, E, D, 2 * D_FF), D ** -0.5),
        "b_gate_up": nrm(ks[22], (L, E, 2 * D_FF), 0.02),
        "w_down": nrm(ks[23], (L, E, D_FF, D), D_FF ** -0.5),
        "b_down": nrm(ks[24], (L, E, D), 0.02),
    }

def reference(x, mem, g_mix, w_in, g_q_diff, g_k_diff, lambda_q1, lambda_k1,
              lambda_q2, lambda_k2, g_subln, conv_w, g_mem, w_mem_kv, g_q_mem,
              g_k_mem, w_branch, w_out, g_ffn, w_router, b_router, w_gate_up,
              b_gate_up, w_down, b_down):
    B, S, D = x.shape
    f32 = jnp.float32
    pos = jnp.arange(S, dtype=f32)
    inv_freq = 1.0 / (ROPE_THETA ** (jnp.arange(0, DIFF_HEAD_DIM, 2, dtype=f32) / DIFF_HEAD_DIM))
    ang = pos[:, None] * inv_freq[None, :]
    cos = jnp.cos(ang)[:, None, None, :].astype(x.dtype)
    sin = jnp.sin(ang)[:, None, None, :].astype(x.dtype)
    split_points = np.cumsum(IN_SIZES)[:-1].tolist()

    for l in range(DEPTH):
        lam_init = 0.8 - 0.6 * math.exp(-0.3 * l)
        h = rmsnorm(x, g_mix[l])
        proj = h @ w_in[l]
        dq, dk, dv, cb, cc, ch, mq, gate_logits = jnp.split(proj, split_points, axis=-1)

        dq = rope(rmsnorm(dq.reshape(B, S, DIFF_HEADS, 2, DIFF_HEAD_DIM), g_q_diff[l]), cos, sin)
        dk = rope(rmsnorm(dk.reshape(B, S, DIFF_HEADS, 2, DIFF_HEAD_DIM), g_k_diff[l]), cos, sin)
        dv = dv.reshape(B, S, DIFF_HEADS, DIFF_V_DIM)
        lam = (jnp.exp(jnp.sum(lambda_q1[l].astype(f32) * lambda_k1[l].astype(f32)))
               - jnp.exp(jnp.sum(lambda_q2[l].astype(f32) * lambda_k2[l].astype(f32)))
               + lam_init)
        a = diff_attention(dq, dk, dv, lam)
        a = rmsnorm(a, g_subln[l]) * (1.0 - lam_init)
        y_diff = a.reshape(B, S, DIFF_WIDTH)

        y_conv = cb * causal_depthwise_conv(cc * ch, conv_w[l])

        y_mem = memory_cross_attention(mq, mem, g_mem[l], w_mem_kv[l], g_q_mem[l], g_k_mem[l])

        branches = jnp.stack([y_diff, y_conv, y_mem], axis=2)
        branch_out = jnp.einsum('bsnc,ncd->bsnd', branches, w_branch[l])
        gates = jax.nn.sigmoid(gate_logits.reshape(B, S, N_BRANCH, D))
        merged = jnp.sum(gates * branch_out, axis=2)
        x = x + merged @ w_out[l]

        x = x + moe(rmsnorm(x, g_ffn[l]), w_router[l], b_router[l], w_gate_up[l],
                    b_gate_up[l], w_down[l], b_down[l])
    return x


_drawn_inputs = setup_inputs


def setup_inputs(seed=0):
    import zlib

    import numpy as np

    out = dict(_drawn_inputs(seed))
    spreads = {}
    factors = {'g_q_diff': 17.004,
     'g_k_diff': 11.87,
     'lambda_k2': 30.594,
     'g_mem': 5.829,
     'g_q_mem': 6.568,
     'g_k_mem': 8.0,
     'b_gate_up': 5.922,
     'b_down': 28.596,
     'lambda_q1': 64.0,
     'lambda_k1': 4.483,
     'g_subln': 8.0,
     'g_ffn': 3.321,
     'b_router': 7.161}
    for name, (base, spread) in spreads.items():
        noise = np.random.default_rng([zlib.crc32(name.encode()), seed]).standard_normal(out[name].shape)
        drawn = base * np.exp(spread * noise) if base else spread * noise
        out[name] = __import__('jax').numpy.asarray(drawn.astype(out[name].dtype))
    for name, factor in factors.items():
        out[name] = (out[name] * factor).astype(out[name].dtype)
    return out
```

```python
from contextlib import ExitStack

import concourse.bass as bass
from concourse import mybir

ALU = mybir.AluOpType
ACT = mybir.ActivationFunctionType
F32 = mybir.dt.float32
F32R = mybir.dt.float32r
I32 = mybir.dt.int32
U32 = mybir.dt.uint32
BF16 = mybir.dt.bfloat16
AX_X = mybir.AxisListType.X

P = 128
D = 1024
SEQ = 256
TT = SEQ // P
KD = D // P
EPS = 1e-6
LAM_INIT = 0.2
SWIGLU_LIMIT = 7.0
SWIGLU_ALPHA = 1.702
NEG = -1e30
N_EXPERTS = 32
TOP_K = 4
PAIRS = N_EXPERTS // 2
SLOT_TOKENS = 64
PASSES = SEQ // SLOT_TOKENS

SLOTS = 12
SLOT_W = 2048
FRONT_UNITS = 40
HALVES = 2 * FRONT_UNITS
PAIR_CHUNKS = 24

V_MIX, V_MEM, V_FFN, V_CONV, V_GQM, V_GKM, V_SUB, V_ROWS = 0, 8, 16, 24, 36, 37, 38, 39

C_TRI, C_IOTA, C_EROW, C_PM, C_EIOTA, C_ONES = 0, 128, 384, 512, 530, 562
C_COLS = 704


TASKS = ["vec", "memT0", "memT1", "xT0", "xT1", "mkT", "mqT", "ms0", "ms1", "mp0", "mav0", "mp1", "mav1", "dqT", "dkT",
         "ds00", "ds01", "da0", "ds10", "dav0", "ds11", "da1", "dav1", "dy0", "dy1", "XT0", "XT1", "XT2", "XT3", "ranks"]


def front_units():
    units = []
    for name in ("mk", "mv", "mq", "dq", "dk", "dv", "cc", "ch", "cb"):
        units += [(name, 0), (name, 1)]
    for i in (2, 1, 0):
        for half in range(2):
            units += [(f"gate{i}", 2 * half), (f"gate{i}", 2 * half + 1), (f"branch{i}", half)]
    units += [("out", n) for n in range(4)]
    return units


def build(nc, x, mem, w_in, w_mem_kv, w_branch, w_out, g_mix, g_mem, g_ffn, conv_w, g_q_mem, g_k_mem,
          g_subln, g_q_diff, g_k_diff, lambda_q1, lambda_k1, lambda_q2, lambda_k2, w_router, b_router,
          w_gate_up, b_gate_up, w_down, b_down, c_front, c_moe, out):
    units = front_units()
    assert len(units) == FRONT_UNITS

    use_of, last_of = [], {}
    n_use = -1
    for h in range(HALVES):
        name = units[h // 2][0]
        if h % 2 == 0 or name.startswith("branch"):
            n_use += 1
        use_of.append(n_use)
        last_of[n_use] = h
    N_USES = n_use + 1

    with ExitStack() as ctx:
        def sem(name):
            return ctx.enter_context(nc.semaphore(name))

        def sb(stack, name, shape, dt=F32):
            return stack.enter_context(nc.sbuf_tensor(name, shape, dt))

        ring = sb(ctx, "ring", [P, SLOTS, SLOT_W])
        acc = sb(ctx, "acc", [P, TT, D])
        ident = sb(ctx, "ident", [P, 256])
        vecT = sb(ctx, "vecT", [P, V_ROWS])
        stat = sb(ctx, "stat", [P, 3, 62])
        att = sb(ctx, "att", [P, 4, 24])
        lam = sb(ctx, "lam", [P, 8])
        flag = sb(ctx, "flag", [1, 1], I32)
        x1sq = sb(ctx, "x1sq", [P, TT, 4])

        with ExitStack() as front:
            u = sb(front, "u", [P, 4, 256])
            cb = sb(front, "cb", [P, 4, 256])
            PT = sb(front, "PT", [P, 1024])
            S = sb(front, "S", [P, 2, 1024])
            T = sb(front, "T", [P, 2, 1024])
            ych = sb(front, "ych", [P, 4, 256], F32R)
            ycl = sb(front, "ycl", [P, 4, 256], F32R)
            R = sb(front, "R", [P, 4, 1024])
            WH = sb(front, "WH", [P, 2, 4, 256], F32R)
            WL = sb(front, "WL", [P, 2, 4, 256], F32R)
            hTh = sb(front, "hTh", [P, KD, SEQ], F32R)
            hTl = sb(front, "hTl", [P, KD, SEQ], F32R)
            mTh = sb(front, "mTh", [P, KD, SEQ], F32R)
            mTl = sb(front, "mTl", [P, KD, SEQ], F32R)
            gqk = sb(front, "gqk", [P, 2, 64])

        with ExitStack() as moe:
            bgu = sb(moe, "bgu", [P, 2 * D])
            cm = sb(moe, "cm", [P, C_COLS])
            wr = sb(moe, "wr", [P, KD, N_EXPERTS])
            br = sb(moe, "br", [P, N_EXPERTS])
            sb(moe, "over_PT", [P, 1024 - C_COLS - KD * N_EXPERTS - N_EXPERTS])
            Y = sb(moe, "Y", [P, 2, 512])
            a = sb(moe, "a", [P, D])
            bguh = sb(moe, "bguh", [P, 2 * D], F32R)
            bgul = sb(moe, "bgul", [P, 2 * D], F32R)
            g1 = sb(moe, "g1", [P, 2, 512])
            u1 = sb(moe, "u1", [P, 2, 512])
            Xh = sb(moe, "Xh", [P, TT, D], F32R)
            Xl = sb(moe, "Xl", [P, TT, D], F32R)
            sg = sb(moe, "sg", [P, 2, 512])
            xg = sb(moe, "xg", [P, KD, P])
            aT = sb(moe, "aT", [P, KD, P])
            sel = sb(moe, "sel", [P, TT, P], F32R)
            gsel = sb(moe, "gsel", [P, TT, P])
            gselT = sb(moe, "gselT", [P, TT, P])
            oh = sb(moe, "oh", [P, P], F32R)
            sb(moe, "over_hT", [P, P + KD * SEQ])
            hT2 = sb(moe, "hT2", [P, KD, SEQ])
            lg = sb(moe, "lg", [P, TT, N_EXPERTS])
            top = sb(moe, "top", [P, TT, 8])
            topi = sb(moe, "topi", [P, TT, 8], U32)
            topf = sb(moe, "topf", [P, TT, 8])
            gate4 = sb(moe, "gate4", [P, TT, TOP_K])
            gst = sb(moe, "gst", [P, TT, 4])
            hot = sb(moe, "hot", [P, TT, 2, TOP_K, N_EXPERTS])
            msk = sb(moe, "msk", [P, TT, N_EXPERTS], BF16)
            cmb = sb(moe, "cmb", [P, 2, P], BF16)
            gd = sb(moe, "gd", [P, TT, P])
            slot = sb(moe, "slot", [P, TT, N_EXPERTS + 2])
            cnt = sb(moe, "cnt", [P, 2])

        U = [ctx.enter_context(nc.psum_tensor(f"U{i}", [P, 512], F32)) for i in range(4)]
        M = [ctx.enter_context(nc.psum_tensor(f"M{i}", [P, 1024], F32)) for i in range(2)]

        landed = [sem(f"landed{i}") for i in range(SLOTS)]
        x_in, mem_in, id_in, vec_in, lam_in, gqk_in, wr_in, cm_in, bgu_in, bdn_in, out_done = (sem(n) for n in (
            "x_in", "mem_in", "id_in", "vec_in", "lam_in", "gqk_in", "wr_in", "cm_in", "bgu_in", "bdn_in",
            "out_done"))
        wh_ready = sem("wh_ready")
        w_ready = sem("w_ready")
        w_used = sem("w_used")
        u_free = [sem(f"u_free{i}") for i in range(4)]
        m_full = [sem(f"m_full{i}") for i in range(2)]
        m_free = [sem(f"m_free{i}") for i in range(2)]
        dve_seq, act_seq = sem("dve_seq"), sem("act_seq")
        eps_ready, ss_ready, sd_ready, sq_ready = (sem(n) for n in ("eps_ready", "ss_ready", "sd_ready", "sq_ready"))
        memn_ready, xn_ready, hi_ready = sem("memn_ready"), sem("xn_ready"), sem("hi_ready")
        heads_ready = sem("heads_ready")
        nmx_ready, p_ready, pn_ready = sem("nmx_ready"), sem("p_ready"), sem("pn_ready")
        ydiff_ready, yconv_ready = sem("ydiff_ready"), sem("yconv_ready")
        lam_sum, lam_exp, lam_ready = sem("lam_sum"), sem("lam_exp"), sem("lam_ready")
        conv_ready, ych_ready = sem("conv_ready"), sem("ych_ready")
        merged_ready, mh_ready, ml_ready = (sem(n) for n in ("merged_ready", "mh_ready", "ml_ready"))
        x1sq_ready, cmb_ready, logits_done, rstd_ready = (
            sem(n) for n in ("x1sq_ready", "cmb_ready", "logits_done", "rstd_ready"))
        pad_ready = sem("pad_ready")
        Xh_ready, Xl_ready = sem("Xh_ready"), sem("Xl_ready")
        top_ready, e_ready, msk_ready, gd_ready, flag_ready = (
            sem(n) for n in ("top_ready", "e_ready", "msk_ready", "gd_ready", "flag_ready"))
        bguh_ready, bgul_ready = sem("bguh_ready"), sem("bgul_ready")
        chunk_used = sem("chunk_used")
        sel_ready, oh_ready, gsel_ready, gather_done, xg_ready = (
            sem(n) for n in ("sel_ready", "oh_ready", "gsel_ready", "gather_done", "xg_ready"))
        gu_done, g1_ready, s_ready, a_ready = (sem(n) for n in ("gu_done", "g1_ready", "s_ready", "a_ready"))
        gt_done, gt_ready, at_done, at_ready = (sem(n) for n in ("gt_done", "gt_ready", "at_done", "at_ready"))
        y_ready, sc_done, sc_free, zero_ready = (sem(n) for n in ("y_ready", "sc_done", "sc_free", "zero_ready"))
        dn_done = sem("dn_done")
        last_done, all_done = sem("last_done"), sem("all_done")

        def wait_full(eng, task):
            j = TASKS.index(task)
            eng.wait_ge(m_full[j % 2], j // 2 + 1)

        def wait_read(eng, task):
            j = TASKS.index(task)
            eng.wait_ge(m_free[j % 2], j // 2 + 1)

        def misc(task):
            return M[TASKS.index(task) % 2]

        def free_sem(task):
            return m_free[TASKS.index(task) % 2]

        DN = [M[0][:, 0:512], M[0][:, 512:1024]]
        C = [M[1][:, 0:512], M[1][:, 512:1024]]
        MISC = [DN[0], DN[1], C[0], C[1]]
        LOGITS = C[1][:, 0:TT * N_EXPERTS]

        def idm():
            return ident[:, 0:P]

        def unit_src(c):
            name, part = units[c]
            if name in ("mk", "mv"):
                col = {"mk": 0, "mv": 512}[name] + 256 * part
                return w_mem_kv[0].rearrange("(k p) n -> p k n", p=P)[:, :, col:col + 256]
            if name.startswith("branch"):
                return w_branch[0, int(name[-1])].rearrange("(k p) n -> p k n", p=P)[:, :, 512 * part:512 * part + 512]
            if name == "out":
                return w_out[0].rearrange("(k p) n -> p k n", p=P)[:, :, 256 * part:256 * part + 256]
            if name.startswith("gate"):
                col = 3584 + 1024 * int(name[-1]) + 256 * part
            else:
                col = {"dq": 0, "dk": 512, "dv": 1024, "cb": 1536, "cc": 2048, "ch": 2560, "mq": 3072}[name] + 256 * part
            return w_in[0].rearrange("(k p) n -> p k n", p=P)[:, :, col:col + 256]

        def half_src(h):
            c, j = divmod(h, 2)
            s = ring[:, c % SLOTS, :]
            if units[c][0].startswith("branch"):
                return s.rearrange("p (k n) -> p k n", k=4)[:, :, 256 * j:256 * j + 256]
            return s.rearrange("p (k n) -> p k n", k=8)[:, 4 * j:4 * j + 4, :]

        def raw(i):
            return R[:, i, :].rearrange("p (t n) -> p t n", t=TT)

        def slot_of(i):
            return (FRONT_UNITS + i) % SLOTS

        def landed_at(n, i):
            return n * (16 * PAIR_CHUNKS // SLOTS) + 16 * ((FRONT_UNITS + i) // SLOTS + 1)

        def pair_chunk(i):
            s = ring[:, slot_of(i), :]
            return s if i < 16 else s.rearrange("p (f n) -> p f n", f=2)

        def wait_product(eng, use):
            eng.wait_ge(w_used, last_of[use] + 1)

        def wait_unit(eng, c):
            eng.wait_ge(u_free[use_of[2 * c] % 4], use_of[2 * c] // 4 + 1)

        def merged(i):
            return R[:, i // 2, (i % 2) * 512:(i % 2) * 512 + 512].rearrange("p (s n) -> p s n", s=2)

        def gates(i):
            return T[:, 0, (i % 2) * 512:(i % 2) * 512 + 512].rearrange("p (s n) -> p s n", s=2)

        def first_unit(name):
            return [n for n, _ in units].index(name)

        def merge_order(name):
            return (first_unit("branch" + name[-1]) - first_unit("branch2")) // 6

        def scratch2(i):
            return S[:, 0, (i % 2) * 512:(i % 2) * 512 + 512].rearrange("p (s n) -> p s n", s=2)

        def bank2(m):
            return m[:, :].rearrange("p (k n) -> p k n", k=4)

        RAW_OF = {"mk": 0, "mv": 1, "mq": 2, "dq": 3, "dk": 0, "dv": 2}
        ST = {"mem": (0, 2), "x": (2, 2), "mk": (4, 8), "mq": (12, 8), "dq": (20, 16), "dk": (36, 16),
              "y0": (52, 4), "y1": (56, 4), "x1": (60, 2)}
        MEM_SCALE, DIFF_SCALE = 128.0 ** -0.5, 64.0 ** -0.5

        block = ctx.enter_context(nc.Block())

        @block.sync
        def _(sp):
            sp.dma_start(S[:, :, :], mem[0].rearrange("(t p) d -> p t d", p=P)).then_inc(mem_in, 16)
            for i, v in enumerate((lambda_q1, lambda_k1, lambda_q2, lambda_k2)):
                sp.dma_start(PT[:, 256 + 64 * i:320 + 64 * i], v.broadcast_to([P, 64])).then_inc(lam_in, 16)
            for i, v in enumerate((g_q_diff, g_k_diff)):
                sp.dma_start(gqk[:, i, :], v.broadcast_to([P, 64])).then_inc(gqk_in, 16)
            sp.dma_start(acc[:, :, :], x[0].rearrange("(t p) d -> p t d", p=P)).then_inc(x_in, 16)
            for c in range(FRONT_UNITS):
                if c >= SLOTS:
                    sp.wait_ge(w_ready, 2 * (c - SLOTS) + 2)
                name = units[c][0]
                k = 4 if name.startswith("branch") else 8
                dst = ring[:, c % SLOTS, :].rearrange("p (k n) -> p k n", k=k)
                sp.dma_start(dst, unit_src(c)).then_inc(landed[c % SLOTS], 16)

            gu = w_gate_up[0].rearrange("e (k p) f -> e p k f", p=P)
            dn = w_down[0].rearrange("e (k p) d -> e p k d", p=P)

            def load(e0, i):
                k, e = divmod(i % 16, 2)
                if i < 16:
                    src = gu[bass.ds(e0 + e, 1), :, k, :].rearrange("a p f -> p (a f)")
                else:
                    src = dn[bass.ds(e0 + e, 1), :, 2 * k:2 * k + 2, :].rearrange("a p k d -> p (a k) d")
                sp.dma_start(pair_chunk(i), src).then_inc(landed[slot_of(i)], 16)

            for i in range(PAIR_CHUNKS):
                if i < SLOTS:
                    sp.wait_ge(w_ready, 2 * (FRONT_UNITS + i - SLOTS) + 2)
                else:
                    sp.wait_ge(chunk_used, i - SLOTS + 1)
                load(0, i)
            with sp.Fori(1, PAIRS) as n:
                for i in range(PAIR_CHUNKS):
                    sp.wait_ge(chunk_used, n * PAIR_CHUNKS + (i - SLOTS + 1))
                    load(2 * n, i)
            sp.wait_ge(flag_ready, 1)
            more = sp.value_load(flag[0:1, 0:1], min_val=0, max_val=1)
            with sp.If(more):
                with sp.Fori(1, PASSES) as b:
                    with sp.Fori(0, PAIRS) as n:
                        for i in range(PAIR_CHUNKS):
                            sp.wait_ge(chunk_used, b * (PAIRS * PAIR_CHUNKS) + n * PAIR_CHUNKS + (i - SLOTS + 1))
                            load(2 * n, i)
            for q in range(4):
                t, hf = q // 2, q % 2
                sp.wait_ge(all_done, q + 1)
                sp.dma_start(out[0, t * P:t * P + P, hf * 512:hf * 512 + 512],
                             acc[:, t, hf * 512:hf * 512 + 512]).then_inc(out_done, 16)
            sp.wait_ge(out_done, 4 * 16)

        @block.gpsimd
        def _(pool):
            pool.wait_ge(yconv_ready, 4)
            nc.gpsimd.memset(bgu[:, :], 0.0).then_inc(pad_ready, 1)
            wait_read(pool, "dav1")
            pool.dma_start(cm[:, :], c_moe[:, :]).then_inc(cm_in, 16)
            pool.dma_start(wr[:, :, :], w_router[0].rearrange("(k p) e -> p k e", p=P)).then_inc(wr_in, 16)
            pool.dma_start(br[:, :], b_router.broadcast_to([P, N_EXPERTS])).then_inc(wr_in, 16)
            pool.wait_ge(pad_ready, 1)
            pool.dma_start(bgu[0:N_EXPERTS, :], b_gate_up[0]).then_inc(bgu_in, 16)
            pool.wait_ge(merged_ready, 12)
            nc.gpsimd.memset(Y[:, :, :], 0.0).then_inc(pad_ready, 1)
            pool.wait_ge(pad_ready, 2)
            pool.dma_start(Y[0:N_EXPERTS, :, :], b_down[0].rearrange("e (h n) -> e h n", h=2)).then_inc(bdn_in, 16)

        @block.tensor
        def _(pe):
            n_begun = [0]

            def begin(task):
                j = TASKS.index(task)
                assert j == n_begun[0]
                n_begun[0] += 1
                if j >= 2:
                    pe.wait_ge(m_free[j % 2], j // 2)
                return M[j % 2]

            def end(task, mm):
                mm.then_inc(m_full[TASKS.index(task) % 2], 1)

            def transpose_act(task, src, k0):
                m = bank2(begin(task))
                for k in range(4):
                    for t in range(TT):
                        mm = pe.transpose(m[:, k, t * P:t * P + P], src[:, t, (k0 + k) * P:(k0 + k + 1) * P], idm())
                end(task, mm)

            def transpose_heads(task, i):
                m = bank2(begin(task))
                for h in range(4):
                    for t in range(TT):
                        mm = pe.transpose(m[:, h, t * P:t * P + P], raw(i)[:, t, h * P:h * P + P], idm())
                end(task, mm)

            def mem_scores(t):
                task = f"ms{t}"
                m = bank2(begin(task))
                for h in range(4):
                    mm = pe.matmul(m[:, h, :], T[:, 1, h * 256 + t * P:h * 256 + t * P + P],
                                   T[:, 0, h * 256:h * 256 + 256], start=True, stop=True)
                end(task, mm)

            def mem_pT(t):
                pe.wait_ge(pn_ready, t + 1)
                m = begin(f"mp{t}")
                for h in range(4):
                    for mt in range(2):
                        mm = pe.transpose(m[:, (2 * h + mt) * P:(2 * h + mt + 1) * P],
                                          S[:, t, h * 256 + mt * P:h * 256 + mt * P + P], idm())
                end(f"mp{t}", mm)

            def mem_av(t):
                wait_read(pe, f"mp{t}")
                for c in range(2):
                    wait_unit(pe, first_unit("mv") + c)
                m = begin(f"mav{t}")
                for h in range(4):
                    for mt in range(2):
                        mm = pe.matmul(m[:, h * P:h * P + P], raw(1)[:, mt, h * P:h * P + P],
                                       PT[:, (2 * h + mt) * P:(2 * h + mt + 1) * P], start=(mt == 0), stop=(mt == 1))
                end(f"mav{t}", mm)

            def diff_scores(t, hp):
                task = f"ds{t}{hp}"
                m = bank2(begin(task))
                for hh in range(2):
                    for c in range(2):
                        h = 2 * hp + hh
                        mm = pe.matmul(m[:, 2 * c + hh, 0:P * (t + 1)],
                                       T[64 * c:64 * c + 64, 1, h * 256 + t * P:h * 256 + t * P + P],
                                       T[64 * c:64 * c + 64, 0, h * 256:h * 256 + P * (t + 1)], start=True, stop=True)
                end(task, mm)

            def diff_aT(t):
                pe.wait_ge(pn_ready, 2 + 2 * t + 2)
                m = begin(f"da{t}")
                for h in range(4):
                    for kt in range(t + 1):
                        i = h * (t + 1) + kt
                        mm = pe.transpose(m[:, i * P:i * P + P],
                                          S[:, h // 2, (h % 2) * 256 + kt * P:(h % 2) * 256 + kt * P + P], idm())
                end(f"da{t}", mm)

            def diff_av(t):
                wait_read(pe, f"da{t}")
                for c in range(2):
                    wait_unit(pe, first_unit("dv") + c)
                m = begin(f"dav{t}")
                for h in range(4):
                    for kt in range(t + 1):
                        i = h * (t + 1) + kt
                        mm = pe.matmul(m[:, h * P:h * P + P], PT[:, i * P:i * P + P],
                                       raw(2)[:, kt, h * P:h * P + P], start=(kt == 0), stop=(kt == t))
                end(f"dav{t}", mm)

            def diff_yT(t):
                pe.wait_ge(ydiff_ready, t + 1)
                m = begin(f"dy{t}")
                for h in range(4):
                    mm = pe.transpose(m[:, h * P:h * P + P], raw(3)[:, t, h * P:h * P + P], idm())
                end(f"dy{t}", mm)

            def half_unit(h):
                c, j = divmod(h, 2)
                name, part = units[c]
                use = use_of[h]
                whole = name.startswith("branch")
                begins, ends = whole or j == 0, whole or j == 1
                bank = U[use % 4][:, :].rearrange("p (s n) -> p s n", s=2)
                if begins and use >= 4:
                    pe.wait_ge(u_free[use % 4], use // 4)
                if part == 0 and j == 0:
                    if name == "mk":
                        wait_read(pe, "memT0")
                        wait_read(pe, "memT1")
                    if name == "mq":
                        wait_read(pe, "xT0")
                        wait_read(pe, "xT1")
                    if name == "branch2":
                        wait_read(pe, "mav0")
                        wait_read(pe, "mav1")
                    if name == "branch1":
                        pe.wait_ge(yconv_ready, 4)
                    if name == "branch0":
                        wait_read(pe, "dy0")
                        wait_read(pe, "dy1")
                if name == "out" and part == 0:
                    pe.wait_ge(ml_ready, 2 * j + 2)
                pe.wait_ge(w_ready, h + 1)
                k0 = 4 * j
                if name in ("mk", "mv"):
                    ah, al = mTh, mTl
                elif name == "branch1":
                    ah, al, k0 = ych, ycl, 0
                elif name == "branch2":
                    ah, al, k0 = mTh, mTl, 0
                elif name == "branch0":
                    ah, al, k0 = mTh, mTl, 4
                else:
                    ah, al = hTh, hTl
                tokens_out = name in ("mk", "mv", "mq", "dq", "dk", "dv", "out")
                for s in range(2):
                    for k in range(4):
                        for q, (aa, ww) in enumerate(((ah, WH), (al, WH), (ah, WL))):
                            if tokens_out:
                                lhsT, rhs = aa[:, k0 + k, s * P:s * P + P], ww[:, h % 2, k, :]
                            else:
                                lhsT, rhs = ww[:, h % 2, k, s * P:s * P + P], aa[:, k0 + k, :]
                            mm = pe.matmul(bank[:, s, :], lhsT, rhs, start=begins and s == 0 and k == 0 and q == 0,
                                           stop=ends and s == 1 and k == 3 and q == 2, skip_group_check=True)
                mm.then_inc(w_used, 1)

            def x1_transposes(n):
                wait_unit(pe, first_unit("out") + n)
                m = begin(f"XT{n}")
                for k in range(2):
                    for t in range(TT):
                        mm = pe.transpose(m[:, (2 * k + t) * P:(2 * k + t) * P + P],
                                          acc[:, t, (2 * n + k) * P:(2 * n + k + 1) * P], idm())
                end(f"XT{n}", mm)

            def logits(n):
                wait_read(pe, f"XT{n}")
                if n == 0:
                    pe.wait_ge(wr_in, 32)
                    wait_read(pe, "dy0")
                for k in (2 * n, 2 * n + 1):
                    for t in range(TT):
                        mm = pe.matmul(LOGITS[:, t * N_EXPERTS:(t + 1) * N_EXPERTS], hT2[:, k, t * P:t * P + P],
                                       wr[:, k, :], start=(k == 0 and t == 0), stop=(k == KD - 1 and t == 1),
                                       skip_group_check=True)
                if n == 3:
                    mm.then_inc(logits_done, 1)

            pe.wait_ge(id_in, 16)
            pe.wait_ge(vec_in, 16 * 7)
            m = begin("vec")
            end("vec", pe.transpose(m[:, 0:V_ROWS], PT[0:V_ROWS, 0:P], ident[0:V_ROWS, 0:V_ROWS]))
            pe.wait_ge(memn_ready, 2)
            transpose_act("memT0", R[:, 0:2, :], 0)
            transpose_act("memT1", R[:, 0:2, :], 4)
            for h in range(HALVES):
                half_unit(h)
                if h == 1:
                    pe.wait_ge(xn_ready, 2)
                    transpose_act("xT0", R[:, 2:4, :], 0)
                    transpose_act("xT1", R[:, 2:4, :], 4)
                if h == 9:
                    pe.wait_ge(heads_ready, 1)
                    transpose_heads("mkT", 0)
                if h == 16:
                    pe.wait_ge(heads_ready, 2)
                    transpose_heads("mqT", 2)
                if h == 18:
                    wait_read(pe, "mkT")
                    wait_read(pe, "mqT")
                    mem_scores(0)
                    mem_scores(1)
                if h == 21:
                    mem_pT(0)
                if h == 23:
                    mem_av(0)
                    mem_pT(1)
                if h == 25:
                    mem_av(1)
                if h == 27:
                    pe.wait_ge(heads_ready, 3)
                    transpose_heads("dqT", 3)
                if h == 29:
                    pe.wait_ge(heads_ready, 4)
                    transpose_heads("dkT", 0)
                if h == 31:
                    wait_read(pe, "dqT")
                    wait_read(pe, "dkT")
                    diff_scores(0, 0)
                    diff_scores(0, 1)
                if h == 35:
                    diff_aT(0)
                    diff_scores(1, 0)
                if h == 37:
                    diff_av(0)
                    diff_scores(1, 1)
                if h == 41:
                    diff_aT(1)
                if h == 43:
                    diff_av(1)
                if h == 47:
                    diff_yT(0)
                if h == 49:
                    diff_yT(1)
                if h == 75:
                    x1_transposes(0)
                if h == 77:
                    x1_transposes(1)
                if h == 78:
                    logits(0)

            x1_transposes(2)
            logits(1)
            x1_transposes(3)
            logits(2)
            logits(3)
            pe.wait_ge(cmb_ready, 1)
            pe.wait_ge(msk_ready, 1)
            tri, ones = cmb[:, 0, :], cmb[:, 1, :]
            m = begin("ranks")
            pe.matmul(m[:, 0:32], tri, msk[:, 0, :], start=True, stop=True)
            pe.matmul(m[:, 32:64], ones, msk[:, 0, :], start=True, stop=False)
            pe.matmul(m[:, 32:64], tri, msk[:, 1, :], start=False, stop=True)
            pe.matmul(m[:, 64:96], ones, msk[:, 0, :], start=True, stop=False)
            end("ranks", pe.matmul(m[:, 64:96], ones, msk[:, 1, :], start=False, stop=True))

            def gather(k):
                pe.wait_ge(sel_ready, k + 1)
                for dh in range(2):
                    for q, xx in enumerate((Xh, Xl)):
                        if isinstance(k, int) and k == 0 and dh == 0 and q == 1:
                            pe.wait_ge(Xl_ready, 2)
                        for dd in range(4):
                            d = 4 * dh + dd
                            for t in range(TT):
                                mm = pe.matmul(DN[dh][:, dd * P:dd * P + P], xx[:, t, d * P:d * P + P], sel[:, t, :],
                                               start=(q == 0 and dd == 0 and t == 0),
                                               stop=(q == 1 and dd == 3 and t == 1), skip_group_check=True)
                    mm.then_inc(gather_done, 1)

            def scatter(signal):
                for q in range(4):
                    t, hf = q // 2, q % 2
                    pe.matmul(MISC[q], gselT[:, t, :], Y[:, hf, :], start=True, stop=True).then_inc(signal, 1)

            def pair(n, k):
                pe.wait_ge(xg_ready, 2 * k + 2)
                for kk in range(KD):
                    for e in range(2):
                        i = 2 * kk + e
                        pe.wait_ge(landed[slot_of(i)], landed_at(n, i))
                    for nb in range(4):
                        for e in range(2):
                            mm = pe.matmul(U[nb][64 * e:64 * e + 64, :], xg[:, kk, 64 * e:64 * e + 64],
                                           pair_chunk(2 * kk + e)[:, nb * 512:nb * 512 + 512],
                                           start=(kk == 0), stop=False, skip_group_check=True)
                            if nb == 3:
                                mm.then_inc(chunk_used, 1)
                pe.wait_ge(oh_ready, k + 1)
                pe.wait_ge(bgul_ready, 1)
                for hf in range(2):
                    for nb in (hf, 2 + hf):
                        for q, bb in enumerate((bguh, bgul)):
                            mm = pe.matmul(U[nb][:, :], oh[:, :], bb[:, nb * 512:nb * 512 + 512],
                                           start=False, stop=(q == 1), skip_group_check=True)
                    mm.then_inc(gu_done, 1)
                pe.wait_ge(y_ready, 2 * n + 2)
                pe.wait_ge(gt_ready, n + 1)
                scatter(sc_done)
                pe.wait_ge(sc_free, 4 * k + 2 + 4)
                gather(k + 1)
                pe.wait_ge(gsel_ready, n + 1)
                pe.wait_ge(sc_free, 4 * k + 4 + 4)
                pe.transpose(C[0][:, 0:P], gsel[:, 0, :], idm())
                pe.transpose(C[0][:, P:2 * P], gsel[:, 1, :], idm()).then_inc(gt_done, 1)
                for hf in range(2):
                    pe.wait_ge(a_ready, 2 * n + hf + 1)
                    if hf == 1:
                        pe.wait_ge(gt_ready, n + 2)
                    for f in range(4):
                        mm = pe.transpose(C[1 - hf][:, f * P:f * P + P], a[:, (4 * hf + f) * P:(4 * hf + f + 1) * P], idm())
                    mm.then_inc(at_done, 1)
                pe.wait_ge(xg_ready, 2 * k + 4)
                for kk in range(4):
                    pe.wait_ge(at_ready, 2 * n + 1 + kk // 2)
                    for e in range(2):
                        i = 16 + 2 * kk + e
                        pe.wait_ge(landed[slot_of(i)], landed_at(n, i))
                    for hf in range(2):
                        for f2 in range(2):
                            f = 2 * kk + f2
                            for e in range(2):
                                mm = pe.matmul(DN[hf][64 * e:64 * e + 64, :], aT[:, f, 64 * e:64 * e + 64],
                                               pair_chunk(16 + 2 * kk + e)[:, f2, hf * 512:hf * 512 + 512],
                                               start=(f == 0), stop=(f == KD - 1), skip_group_check=True)
                                if f2 == 1 and hf == 1:
                                    mm.then_inc(chunk_used, 1)
                                elif f2 == 1 and kk == 3 and e == 1:
                                    mm.then_inc(dn_done, 1)

            def pairs(n0, k0):
                with pe.Fori(0, PAIRS) as p:
                    pair(n0 + p, k0 + p)
                pe.wait_ge(y_ready, n0 * 2 + (2 * PAIRS + 2))
                pe.wait_ge(gt_ready, n0 + (PAIRS + 1))

            pe.wait_ge(Xh_ready, 2)
            gather(0)
            pe.wait_ge(gd_ready, 1)
            wait_read(pe, "ranks")
            pe.transpose(C[0][:, 0:P], gd[:, 0, :], idm())
            pe.transpose(C[0][:, P:2 * P], gd[:, 1, :], idm()).then_inc(gt_done, 1)
            for q in range(4):
                pe.wait_ge(u_free[(N_USES - 4 + q) % 4], (N_USES - 4 + q) // 4 + 1)
            pe.wait_ge(bdn_in, 16)
            pairs(0, 0)
            pe.wait_ge(flag_ready, 1)
            more = pe.value_load(flag[0:1, 0:1], min_val=0, max_val=1)
            with pe.If(more):
                with pe.Fori(1, PASSES) as b:
                    scatter(sc_done)
                    pe.wait_ge(sc_free, b * (PAIRS + 1) * 4 + 4)
                    pe.wait_ge(zero_ready, b)
                    gather(b * (PAIRS + 1))
                    pairs(b * PAIRS, b * (PAIRS + 1))
            scatter(last_done)

        @block.scalar
        def _(act):
            n_own = [0]

            def link(ins):
                n_own[0] += 1
                ins.then_inc(act_seq, 1)
                act.wait_ge(act_seq, n_own[0])

            def split_hi(h):
                if h >= 2:
                    act.wait_ge(w_used, h - 1)
                act.wait_ge(landed[(h // 2) % SLOTS], 16 * (h // 2 // SLOTS + 1))
                act.copy(WH[:, h % 2], half_src(h)).then_inc(wh_ready, 1)

            def rms_rows(src, name, in_sem, count, junk):
                at, n = ST[name]
                act.wait_ge(in_sem, count)
                for t in range(TT):
                    act.activation(junk[:, t, :], src[:, t, :], ACT.Square,
                                   accum_out=stat[:, 0, at + t:at + t + 1]).then_inc(act_seq, 1)
                    n_own[0] += 1
                act.wait_ge(act_seq, n_own[0])
                act.activation(stat[:, 1, at:at + n], stat[:, 0, at:at + n], ACT.Sqrt, bias=lam[:, 6:7],
                               scale=1.0 / D).then_inc(sd_ready, 1)

            def rms_heads(name, dim, count):
                at, n = ST[name]
                act.wait_ge(ss_ready, count)
                act.activation(stat[:, 1, at:at + n], stat[:, 0, at:at + n], ACT.Sqrt, bias=lam[:, 6:7],
                               scale=1.0 / dim).then_inc(sd_ready, 1)

            def hi_of(task, dst, k0, row):
                wait_full(act, task)
                for k in range(4):
                    ins = act.activation(dst[:, k0 + k, :], bank2(misc(task))[:, k, :], ACT.Copy,
                                         scale=vecT[:, row + k0 + k:row + k0 + k + 1])
                ins.then_inc(hi_ready, 1)

            def evac(use, dst, func=ACT.Copy):
                wait_product(act, use)
                act.activation(dst, U[use % 4][:, :].rearrange("p (s n) -> p s n", s=2),
                               func).then_inc(u_free[use % 4], 1)

            def squares(i, name):
                for c in range(2):
                    wait_unit(act, first_unit(name) + c)
                act.activation(cb[:, :, :].rearrange("p a b -> p (a b)"), R[:, i, :], ACT.Square).then_inc(sq_ready, 1)

            def x1_squares(n):
                wait_unit(act, first_unit("out") + n)
                for t in range(TT):
                    act.activation(R[:, 2 + t, 256 * n:256 * n + 256], acc[:, t, 256 * n:256 * n + 256], ACT.Square,
                                   accum_out=x1sq[:, t, n:n + 1]).then_inc(x1sq_ready, 1)

            def squares_y(t):
                wait_read(act, f"dav{t}")
                act.activation(T[:, 1, 512 * t:512 * t + 512], R[:, 3, 512 * t:512 * t + 512],
                               ACT.Square).then_inc(sq_ready, 1)

            def exps(g, task, keys, scale, dst):
                act.wait_ge(nmx_ready, g + 1)
                m = bank2(misc(task))
                for i in range(4):
                    ins = act.activation(dst[:, i, 0:keys], m[:, i, 0:keys], ACT.Exp, scale=scale,
                                         bias=att[:, 1, 4 * g + i:4 * g + i + 1],
                                         accum_out=att[:, 2, 4 * g + i:4 * g + i + 1])
                ins.then_inc(p_ready, 1)

            def to_sbuf(task, dst, cols):
                wait_full(act, task)
                act.copy(dst, misc(task)[:, 0:cols]).then_inc(free_sem(task), 1)

            def hi_y(task, dst, scale):
                wait_full(act, task)
                act.activation(dst, misc(task)[:, 0:512].rearrange("p (h q) -> p h q", h=4), ACT.Copy,
                               scale=scale).then_inc(hi_ready, 1)

            S4 = [S[:, i, :].rearrange("p (m k) -> p m k", m=4) for i in range(2)]

            def rows(v):
                return v.rearrange("a (k p) -> (a k) p", p=P)

            act.dma_start(ident[:, :], c_front[:, :]).then_inc(id_in, 16)
            for at, n, v in ((V_MIX, 8, g_mix), (V_MEM, 8, g_mem), (V_FFN, 8, g_ffn), (V_GQM, 1, g_q_mem),
                             (V_GKM, 1, g_k_mem), (V_SUB, 1, g_subln)):
                act.dma_start(PT[at:at + n, 0:P], rows(v)).then_inc(vec_in, 16)
            act.dma_start(PT[V_CONV:V_CONV + 12, 0:P],
                          conv_w[0].rearrange("j (k p) -> (j k) p", p=P)).then_inc(vec_in, 16)
            act.wait_ge(eps_ready, 1)
            act.activation(lam[:, 7:8], lam[:, 6:7], ACT.Sqrt)
            rms_rows(S, "mem", mem_in, 16, T)
            split_hi(0)
            split_hi(1)
            wait_read(act, "vec")
            hi_of("memT0", mTh, 0, V_MEM)
            hi_of("memT1", mTh, 4, V_MEM)
            rms_rows(acc, "x", x_in, 16, T)
            for h in range(2, HALVES):
                split_hi(h)
                if h == 3:
                    hi_of("xT0", hTh, 0, V_MIX)
                    hi_of("xT1", hTh, 4, V_MIX)
                if h % 2 == 1:
                    c = (h - 3) // 2
                    name, part = units[c]
                    if name in RAW_OF:
                        evac(c, raw(RAW_OF[name])[:, :, 256 * part:256 * part + 256])
                    elif name == "cc":
                        evac(c, u[:, 2 * part:2 * part + 2, :])
                    elif name == "cb":
                        evac(c, cb[:, 2 * part:2 * part + 2, :])
                    elif name.startswith("gate"):
                        if c == first_unit("gate2"):
                            wait_full(act, "ds11")
                        used = 4 * merge_order(name) + part - 1
                        if used > 0:
                            act.wait_ge(merged_ready, used)
                        evac(use_of[2 * c], gates(part), ACT.Sigmoid)
                if h == 5:
                    act.wait_ge(lam_sum, 1)
                    act.activation(lam[:, 2:4], lam[:, 0:2], ACT.Exp).then_inc(lam_exp, 1)
                    squares(0, "mk")
                if h == 7:
                    rms_heads("mk", 128, 1)
                if h == 13:
                    squares(2, "mq")
                if h == 15:
                    rms_heads("mq", 128, 2)
                if h == 17:
                    squares(3, "dq")
                if h == 19:
                    rms_heads("dq", 64, 3)
                if h == 20:
                    exps(0, "ms0", 256, MEM_SCALE, S4[0])
                if h == 21:
                    exps(1, "ms1", 256, MEM_SCALE, S4[1])
                if h == 23:
                    to_sbuf("mp0", PT[:, :], 1024)
                    act.wait_ge(heads_ready, 3)
                    squares(0, "dk")
                if h == 25:
                    rms_heads("dk", 64, 4)
                    hi_y("mav0", mTh[:, 0:4, 0:P], 1.0)
                    to_sbuf("mp1", PT[:, :], 1024)
                if h == 27:
                    hi_y("mav1", mTh[:, 0:4, P:2 * P], 1.0)
                if h == 29:
                    to_sbuf("dqT", T[:, 1, :], 1024)
                if h == 31:
                    to_sbuf("dkT", T[:, 0, :], 1024)
                if h == 33:
                    exps(2, "ds00", 128, DIFF_SCALE, S4[0])
                if h == 34:
                    exps(3, "ds01", 128, DIFF_SCALE, S4[1])
                if h == 37:
                    to_sbuf("da0", PT[:, 0:512], 512)
                    exps(4, "ds10", 256, DIFF_SCALE, S4[0])
                if h == 39:
                    to_sbuf("dav0", R[:, 3, 0:512], 512)
                    exps(5, "ds11", 256, DIFF_SCALE, S4[1])
                if h == 40:
                    squares_y(0)
                if h == 42:
                    rms_heads("y0", 128, 5)
                if h == 43:
                    to_sbuf("da1", PT[:, :], 1024)
                if h == 45:
                    to_sbuf("dav1", R[:, 3, 512:1024], 512)
                if h == 46:
                    squares_y(1)
                if h == 48:
                    rms_heads("y1", 128, 6)
                if 45 <= h <= 48:
                    k = h - 45
                    act.wait_ge(conv_ready, k + 1)
                    act.copy(ych[:, k, :], S[:, 1, 256 * k:256 * k + 256]).then_inc(ych_ready, 1)
                if h == 49:
                    act.wait_ge(lam_ready, 1)
                    hi_y("dy0", mTh[:, 4:8, 0:P], lam[:, 5:6])
                if h == 51:
                    hi_y("dy1", mTh[:, 4:8, P:2 * P], lam[:, 5:6])
                if h in (72, 73):
                    for i in (2 * (h - 72), 2 * (h - 72) + 1):
                        act.wait_ge(merged_ready, 9 + i)
                        act.copy(hTh[:, 2 * i:2 * i + 2, :], merged(i)).then_inc(mh_ready, 1)
                if h == 74:
                    act.activation(lam[:, 7:8], lam[:, 6:7], ACT.Sqrt)
                    act.wait_ge(cm_in, 16)
                    act.copy(cmb[:, 0, :], cm[:, C_TRI:C_TRI + P])
                    act.copy(cmb[:, 1, :], cm[:, C_ONES:C_ONES + P]).then_inc(cmb_ready, 1)
                if h in (75, 77):
                    act.wait_ge(bgu_in, 16)
                    act.wait_ge(merged_ready, 12)
                    v = slice(D * (h - 75) // 2, D * (h - 75) // 2 + D)
                    act.copy(bguh[:, v], bgu[:, v]).then_inc(bguh_ready, 1)
                if h == 76:
                    x1_squares(0)
                if h == 78:
                    x1_squares(1)

            x1_squares(2)
            x1_squares(3)
            rms_heads("x1", D, 7)
            act.wait_ge(rstd_ready, 1)
            at, _n = ST["x1"]
            for t in range(TT):
                act.activation(Xh[:, t, :], acc[:, t, :], ACT.Copy,
                               scale=stat[:, 2, at + t:at + t + 1]).then_inc(Xh_ready, 1)
            act.wait_ge(top_ready, 1)
            for t in range(TT):
                ins = act.activation(gate4[:, t, :], top[:, t, 0:TOP_K], ACT.Exp, bias=gst[:, t, 0:1],
                                     accum_out=gst[:, t, 1:2])
            ins.then_inc(e_ready, 1)
            act.wait_ge(gt_done, 1)
            act.copy(gselT[:, :, :].rearrange("p t n -> p (t n)"), C[0][:, 0:2 * P]).then_inc(gt_ready, 1)
            act.sem_inc(y_ready, 2)

            def pair(n):
                for hf in range(2):
                    act.wait_ge(g1_ready, 2 * n + hf + 1)
                    act.activation(sg[:, hf, :], g1[:, hf, :], ACT.Sigmoid, scale=SWIGLU_ALPHA).then_inc(s_ready, 1)
                act.wait_ge(gt_done, n + 2)
                act.copy(gselT[:, :, :].rearrange("p t n -> p (t n)"), C[0][:, 0:2 * P]).then_inc(gt_ready, 1)
                for hf in range(2):
                    act.wait_ge(at_done, 2 * n + hf + 1)
                    act.copy(aT[:, 4 * hf:4 * hf + 4, :].rearrange("p f n -> p (f n)"), C[1 - hf]).then_inc(at_ready, 1)
                act.wait_ge(dn_done, n + 1)
                act.copy(Y[:, 0, :], DN[0]).then_inc(y_ready, 1)

            with act.Fori(0, PAIRS) as p:
                pair(p)
            act.wait_ge(flag_ready, 1)
            more = act.value_load(flag[0:1, 0:1], min_val=0, max_val=1)
            with act.If(more):
                with act.Fori(1, PASSES) as b:
                    with act.Fori(0, PAIRS) as p:
                        pair(b * PAIRS + p)
            act.nop()

        @block.vector
        def _(dve):
            n_own = [0]

            def link(ins):
                n_own[0] += 1
                ins.then_inc(dve_seq, 1)
                dve.wait_ge(dve_seq, n_own[0])

            def split_lo(h):
                dve.wait_ge(wh_ready, h + 1)
                dve.tensor_tensor(WL[:, h % 2], half_src(h), WH[:, h % 2].bitcast(F32), ALU.subtract).then_inc(w_ready, 1)

            def inverse(name, order):
                at, n = ST[name]
                dve.wait_ge(sd_ready, order)
                link(dve.reciprocal(stat[:, 2, at:at + n], stat[:, 1, at:at + n]))

            def scale_rows(dst, src, name, signal):
                at, _n = ST[name]
                for t in range(TT):
                    dve.tensor_scalar(dst[:, t, :], src[:, t, :], stat[:, 2, at + t:at + t + 1], None,
                                      ALU.mult).then_inc(signal, 1)

            def lo_of(task, order, dst, hi, k0, row):
                dve.wait_ge(hi_ready, order)
                for k in range(4):
                    ins = dve.scalar_tensor_tensor(
                        out=dst[:, k0 + k, :], in0=bank2(misc(task))[:, k, :],
                        scalar=vecT[:, row + k0 + k:row + k0 + k + 1],
                        in1=hi[:, k0 + k, :].bitcast(F32), op0=ALU.mult, op1=ALU.subtract)
                ins.then_inc(free_sem(task), 1)

            def lo_y(task, order, dst, hi, scale):
                dve.wait_ge(hi_ready, order)
                dve.scalar_tensor_tensor(
                    out=dst, in0=misc(task)[:, 0:512].rearrange("p (h q) -> p h q", h=4), scalar=scale,
                    in1=hi.bitcast(F32), op0=ALU.mult, op1=ALU.subtract).then_inc(free_sem(task), 1)

            def head_sums(name, order, src, dim):
                at, n = ST[name]
                dve.wait_ge(sq_ready, order)
                dve.tensor_reduce(stat[:, 0, at:at + n], src.rearrange("p (g n) -> p g n", n=dim), AX_X,
                                  ALU.add).then_inc(ss_ready, 1)

            def head_norm(name, order, v, dim):
                at, n = ST[name]
                inverse(name, order)
                w = v.rearrange("p (g n) -> p g n", n=dim)
                return dve.tensor_tensor(w, w, stat[:, 2, at:at + n].unsqueeze(2).broadcast_to([P, n, dim]), ALU.mult)

            def gains(i, which):
                w = R[:, i, :].rearrange("p (g n) -> p g n", n=64)
                link(dve.tensor_tensor(w, w, gqk[:, which, :].unsqueeze(1).broadcast_to([P, 16, 64]), ALU.mult))

            def rope(i):
                v = R[:, i, :].rearrange("p (t g n) -> p t g n", t=TT, g=8)
                x1, x2 = v[:, :, :, 0:32], v[:, :, :, 32:64]
                tab = ident[:, P:2 * P].rearrange("p (t c n) -> p t c n", t=TT, c=2)
                cos, sin = (tab[:, :, c, :].unsqueeze(2).broadcast_to([P, TT, 8, 32]) for c in range(2))
                prod = cb[:, :, :].rearrange("p a b -> p (a b)").rearrange("p (c t g n) -> p c t g n", c=2, t=TT, g=8)
                dve.tensor_tensor(prod[:, 0], x1, cos, ALU.mult)
                link(dve.tensor_tensor(prod[:, 1], x1, sin, ALU.mult))
                dve.tensor_tensor(x1, x2, sin, ALU.mult)
                link(dve.tensor_tensor(x2, x2, cos, ALU.mult))
                dve.tensor_tensor(x1, prod[:, 0], x1, ALU.subtract)
                dve.tensor_tensor(x2, x2, prod[:, 1], ALU.add).then_inc(heads_ready, 1)

            def softmax_max(g, task, keys, scale, mask_from=None):
                wait_full(dve, task)
                m = bank2(misc(task))
                if mask_from is not None:
                    link(dve.memset(m[0:64, :, mask_from:mask_from + 64], NEG))
                link(dve.tensor_reduce(att[:, 0, 4 * g:4 * g + 4], m[:, :, 0:keys], AX_X, ALU.max))
                dve.tensor_scalar(att[:, 1, 4 * g:4 * g + 4], att[:, 0, 4 * g:4 * g + 4], -scale, None,
                                  ALU.mult).then_inc(nmx_ready, 1)

            def softmax_norm(g, task, keys, v, diff):
                dve.wait_ge(p_ready, g + 1)
                r = att[:, 3, 4 * g:4 * g + 4]
                link(dve.reciprocal(r, att[:, 2, 4 * g:4 * g + 4]))
                if diff:
                    r2 = r[:, 2:4]
                    link(dve.tensor_scalar(r2, r2, lam[:, 4:5], None, ALU.mult))
                w = v[:, :, 0:keys]
                ins = dve.tensor_tensor(w, w, r.unsqueeze(2).broadcast_to([P, 4, keys]), ALU.mult)
                if diff:
                    link(ins)
                    ins = dve.tensor_tensor(w[:, 0:2, :], w[:, 0:2, :], w[:, 2:4, :], ALU.add)
                ins.then_inc(pn_ready, 1)
                dve.wait_ge(pn_ready, g + 1)
                dve.sem_inc(free_sem(task), 1)

            def conv_chunk(k):
                y = S[:, 1, 256 * k:256 * k + 256]
                w = [vecT[:, V_CONV + 4 * j + k:V_CONV + 4 * j + k + 1] for j in range(3)]
                link(dve.tensor_scalar(y, u[:, k, :], w[2], None, ALU.mult))
                for j in (1, 0):
                    d = 2 - j
                    link(dve.scalar_tensor_tensor(out=y[:, d:256], in0=u[:, k, 0:256 - d], scalar=w[j],
                                                  in1=y[:, d:256], op0=ALU.mult, op1=ALU.add))
                dve.tensor_tensor(y, y, cb[:, k, :], ALU.mult).then_inc(conv_ready, 1)

            def x1_channels(n):
                wait_full(dve, f"XT{n}")
                dve.tensor_tensor(hT2[:, 2 * n:2 * n + 2, :], misc(f"XT{n}")[:, 0:512].rearrange("p (k n) -> p k n", k=2),
                                  vecT[:, V_FFN + 2 * n:V_FFN + 2 * n + 2].unsqueeze(2).broadcast_to([P, 2, SEQ]),
                                  ALU.mult).then_inc(free_sem(f"XT{n}"), 1)

            def x_lo(t):
                dve.wait_ge(Xh_ready, t + 1)
                dve.scalar_tensor_tensor(out=Xl[:, t, :], in0=acc[:, t, :], scalar=stat[:, 2, ST["x1"][0] + t:ST["x1"][0] + t + 1],
                                         in1=Xh[:, t, :].bitcast(F32), op0=ALU.mult, op1=ALU.subtract).then_inc(Xl_ready, 1)

            S4 = [S[:, i, :].rearrange("p (m k) -> p m k", m=4) for i in range(2)]

            dve.memset(lam[:, 6:7], EPS).then_inc(eps_ready, 1)
            wait_full(dve, "vec")
            dve.tensor_copy(vecT[:, :], misc("vec")[:, 0:V_ROWS]).then_inc(free_sem("vec"), 1)
            inverse("mem", 1)
            scale_rows(R[:, 0:2, :], S, "mem", memn_ready)
            split_lo(0)
            split_lo(1)
            wait_read(dve, "vec")
            lo_of("memT0", 1, mTl, mTh, 0, V_MEM)
            lo_of("memT1", 2, mTl, mTh, 4, V_MEM)
            inverse("x", 2)
            scale_rows(R[:, 2:4, :], acc, "x", xn_ready)
            dve.wait_ge(lam_in, 64)
            for i in range(2):
                ll = PT[:, 256 + 128 * i:384 + 128 * i]
                ins = dve.tensor_tensor(u[:, i, 0:64], ll[:, 0:64], ll[:, 64:128], ALU.mult)
            link(ins)
            dve.tensor_reduce(lam[:, 0:2], u[:, 0:2, 0:64], AX_X, ALU.add).then_inc(lam_sum, 1)
            dve.tensor_scalar(lam[:, 5:6], vecT[:, V_SUB:V_SUB + 1], 1.0 - LAM_INIT, None, ALU.mult).then_inc(lam_ready, 1)

            for h in range(2, HALVES + 2):
                if h < HALVES:
                    split_lo(h)
                if h == 3:
                    lo_of("xT0", 3, hTl, hTh, 0, V_MIX)
                    lo_of("xT1", 4, hTl, hTh, 4, V_MIX)
                    dve.wait_ge(gqk_in, 32)
                name, part = units[(h - 2) // 2]
                if name.startswith("branch"):
                    use, b, i = use_of[h - 2], merge_order(name), 2 * part + h % 2
                    wait_product(dve, use)
                    wait_unit(dve, first_unit("gate" + name[-1]) + [0, 1, 3, 4][i])
                    if b == 0 and i == 0:
                        wait_full(dve, "mav1")
                    dst = merged(i) if b == 0 else scratch2(i)
                    ins = dve.tensor_tensor(dst, U[use % 4][:, :].rearrange("p (s n) -> p s n", s=2), gates(i), ALU.mult)
                    ins.then_inc(u_free[use % 4], 1)
                    dve.wait_ge(u_free[use % 4], use // 4 + 1)
                    if b == 0:
                        dve.sem_inc(merged_ready, 1)
                    else:
                        dve.tensor_tensor(merged(i), merged(i), scratch2(i), ALU.add).then_inc(merged_ready, 1)
                if h % 2 == 1:
                    c = (h - 3) // 2
                    name, part = units[c]
                    if name == "ch":
                        wait_product(dve, c)
                        wait_unit(dve, first_unit("cc") + part)
                        v = u[:, 2 * part:2 * part + 2, :]
                        dve.tensor_tensor(v, U[c % 4][:, :].rearrange("p (s n) -> p s n", s=2), v,
                                          ALU.mult).then_inc(u_free[c % 4], 1)
                    if name == "out":
                        use = use_of[2 * c]
                        wait_product(dve, use)
                        v = acc[:, :, 256 * part:256 * part + 256]
                        dve.tensor_tensor(v, U[use % 4][:, :].rearrange("p (s n) -> p s n", s=2), v,
                                          ALU.add).then_inc(u_free[use % 4], 1)
                cbv = cb[:, :, :].rearrange("p a b -> p (a b)")
                if h == 6:
                    head_sums("mk", 1, cbv, 128)
                if h == 7:
                    dve.wait_ge(lam_exp, 1)
                    link(dve.scalar_tensor_tensor(out=lam[:, 4:5], in0=lam[:, 3:4], scalar=-LAM_INIT, in1=lam[:, 2:3],
                                                  op0=ALU.add, op1=ALU.subtract))
                    head_norm("mk", 3, R[:, 0, :], 128).then_inc(heads_ready, 1)
                if h == 11:
                    wait_full(dve, "mkT")
                    dve.tensor_scalar(T[:, 0, :], misc("mkT")[:, :], vecT[:, V_GKM:V_GKM + 1], None,
                                      ALU.mult).then_inc(free_sem("mkT"), 1)
                if h == 14:
                    head_sums("mq", 2, cbv, 128)
                if h == 15:
                    head_norm("mq", 4, R[:, 2, :], 128).then_inc(heads_ready, 1)
                if h == 18:
                    wait_full(dve, "mqT")
                    dve.tensor_scalar(T[:, 1, :], misc("mqT")[:, :], vecT[:, V_GQM:V_GQM + 1], None,
                                      ALU.mult).then_inc(free_sem("mqT"), 1)
                    head_sums("dq", 3, cbv, 64)
                if h == 19:
                    softmax_max(0, "ms0", 256, MEM_SCALE)
                    link(head_norm("dq", 5, R[:, 3, :], 64))
                if h == 20:
                    softmax_max(1, "ms1", 256, MEM_SCALE)
                    gains(3, 0)
                if h == 21:
                    softmax_norm(0, "ms0", 256, S4[0], False)
                    rope(3)
                if h == 22:
                    softmax_norm(1, "ms1", 256, S4[1], False)
                if h == 24:
                    head_sums("dk", 4, cbv, 64)
                if h == 25:
                    lo_y("mav0", 5, mTl[:, 0:4, 0:P], mTh[:, 0:4, 0:P], 1.0)
                    link(head_norm("dk", 6, R[:, 0, :], 64))
                if h == 26:
                    gains(0, 1)
                    rope(0)
                if h == 27:
                    lo_y("mav1", 6, mTl[:, 0:4, P:2 * P], mTh[:, 0:4, P:2 * P], 1.0)
                if h == 33:
                    softmax_max(2, "ds00", 128, DIFF_SCALE, 64)
                    softmax_max(3, "ds01", 128, DIFF_SCALE, 64)
                if h == 34:
                    softmax_norm(2, "ds00", 128, S4[0], True)
                if h == 35:
                    softmax_norm(3, "ds01", 128, S4[1], True)
                if h == 37:
                    softmax_max(4, "ds10", 256, DIFF_SCALE, 192)
                if h == 38:
                    softmax_norm(4, "ds10", 256, S4[0], True)
                if h == 39:
                    softmax_max(5, "ds11", 256, DIFF_SCALE, 192)
                if h == 40:
                    softmax_norm(5, "ds11", 256, S4[1], True)
                if h == 41:
                    head_sums("y0", 5, T[:, 1, 0:512], 128)
                if h == 43:
                    head_norm("y0", 7, R[:, 3, 0:512], 128).then_inc(ydiff_ready, 1)
                if 44 <= h <= 47:
                    if h == 44:
                        wait_full(dve, "da1")
                        for c in range(2):
                            wait_unit(dve, first_unit("cb") + c)
                    conv_chunk(h - 44)
                if 46 <= h <= 49:
                    k = h - 46
                    dve.wait_ge(ych_ready, k + 1)
                    dve.tensor_tensor(ycl[:, k, :], S[:, 1, 256 * k:256 * k + 256], ych[:, k, :].bitcast(F32),
                                      ALU.subtract).then_inc(yconv_ready, 1)
                if h == 47:
                    head_sums("y1", 6, T[:, 1, 512:1024], 128)
                if h == 49:
                    head_norm("y1", 8, R[:, 3, 512:1024], 128).then_inc(ydiff_ready, 1)
                    lo_y("dy0", 7, mTl[:, 4:8, 0:P], mTh[:, 4:8, 0:P], lam[:, 5:6])
                if h == 51:
                    lo_y("dy1", 8, mTl[:, 4:8, P:2 * P], mTh[:, 4:8, P:2 * P], lam[:, 5:6])
                if h == 76:
                    dve.memset(gd[:, :, :], 0.0)
                    link(dve.memset(slot[:, :, N_EXPERTS:N_EXPERTS + 2], -1.0))
                if h in (78, 80, 81):
                    x1_channels({78: 0, 80: 1, 81: 2}[h])
                if h in (72, 73):
                    for i in (2 * (h - 72), 2 * (h - 72) + 1):
                        dve.wait_ge(mh_ready, i + 1)
                        dve.tensor_tensor(hTl[:, 2 * i:2 * i + 2, :], merged(i), hTh[:, 2 * i:2 * i + 2, :].bitcast(F32),
                                          ALU.subtract).then_inc(ml_ready, 1)

            at, n = ST["x1"]
            dve.wait_ge(x1sq_ready, 4 * TT)
            dve.tensor_reduce(stat[:, 0, at:at + n], x1sq[:, :, :], AX_X, ALU.add).then_inc(ss_ready, 1)
            x1_channels(3)
            inverse("x1", 9)
            dve.sem_inc(rstd_ready, 1)
            dve.wait_ge(wr_in, 32)
            dve.wait_ge(cm_in, 16)
            dve.wait_ge(logits_done, 1)
            for t in range(TT):
                ins = dve.scalar_tensor_tensor(out=lg[:, t, :], in0=LOGITS[:, t * N_EXPERTS:(t + 1) * N_EXPERTS],
                                               scalar=stat[:, 2, at + t:at + t + 1], in1=br[:, :],
                                               op0=ALU.mult, op1=ALU.add)
            link(ins)
            dve.max(top[:, 0, :], lg[:, 0, :])
            link(dve.max(top[:, 1, :], lg[:, 1, :]))
            dve.tensor_scalar(gst[:, :, 0], top[:, :, 0], -1.0, None, ALU.mult).then_inc(top_ready, 1)
            dve.max_index(topi[:, 0, :], top[:, 0, :], lg[:, 0, :])
            link(dve.max_index(topi[:, 1, :], top[:, 1, :], lg[:, 1, :]))
            link(dve.tensor_copy(topf[:, :, :], topi[:, :, :]))
            every = [P, TT, TOP_K, N_EXPERTS]
            link(dve.tensor_tensor(hot[:, :, 0], cm[:, C_EIOTA:C_EIOTA + N_EXPERTS].unsqueeze(1).unsqueeze(1).broadcast_to(every),
                                   topf[:, :, 0:TOP_K].unsqueeze(3).broadcast_to(every), ALU.is_equal))
            with nc.allow_low_precision(reason="the four indices differ: the sums are 0 or 1"):
                dve.tensor_reduce(msk[:, :, :], hot[:, :, 0].rearrange("p t j e -> p t e j"), AX_X,
                                  ALU.add).then_inc(msk_ready, 1)
            x_lo(0)
            wait_full(dve, "ranks")
            dve.wait_ge(msk_ready, 1)
            m = misc("ranks")
            link(dve.scalar_tensor_tensor(out=slot[:, :, 0:N_EXPERTS], in0=m[:, 0:64].rearrange("p (t e) -> p t e", t=TT),
                                          scalar=1.0, in1=msk[:, :, :], op0=ALU.add, op1=ALU.mult))
            link(dve.tensor_scalar(slot[:, :, 0:N_EXPERTS], slot[:, :, 0:N_EXPERTS], -1.0, None, ALU.add))

            def onehots(p, b, n_gathered):
                if not (isinstance(n_gathered, int) and n_gathered == 0):
                    dve.wait_ge(gather_done, 2 * n_gathered)
                iota = cm[:, bass.ds(C_IOTA + b * SLOT_TOKENS, SLOT_TOKENS)].unsqueeze(1).broadcast_to([P, 2, SLOT_TOKENS])
                for t in range(TT):
                    ins = dve.tensor_tensor(
                        sel[:, t, :].rearrange("p (e s) -> p e s", e=2), iota,
                        slot[:, t, bass.ds(2 * p, 2)].unsqueeze(2).broadcast_to([P, 2, SLOT_TOKENS]), ALU.is_equal)
                ins.then_inc(sel_ready, 1)

            def bias_rows(p):
                dve.tensor_tensor(oh[:, :], cm[:, C_EROW:C_EROW + P],
                                  cm[:, bass.ds(C_PM + p, 1)].broadcast_to([P, P]), ALU.is_equal).then_inc(oh_ready, 1)

            def gathered(k):
                for dh in range(2):
                    dve.wait_ge(gather_done, 2 * k + dh + 1)
                    dve.tensor_tensor(xg[:, 4 * dh:4 * dh + 4, :], DN[dh].rearrange("p (d s) -> p d s", d=4),
                                      vecT[:, V_FFN + 4 * dh:V_FFN + 4 * dh + 4].unsqueeze(2).broadcast_to([P, 4, P]),
                                      ALU.mult).then_inc(xg_ready, 1)

            def add_out(q, k):
                t, hf = q // 2, q % 2
                dve.wait_ge(sc_done, 4 * k + q + 1)
                dve.wait_ge(sc_free, 4 * k + q + 1)
                v = acc[:, t, 512 * hf:512 * hf + 512]
                dve.tensor_tensor(v, MISC[q], v, ALU.add).then_inc(sc_free, 1)

            def swiglu(n, hf, seq):
                dve.wait_ge(gu_done, 2 * n + hf + 1)
                dve.tensor_scalar(g1[:, hf, :], U[hf][:, :], SWIGLU_LIMIT, None, ALU.min).then_inc(g1_ready, 1)
                dve.tensor_scalar(u1[:, hf, :], U[2 + hf][:, :], SWIGLU_LIMIT, -SWIGLU_LIMIT, ALU.min,
                                  ALU.max).then_inc(dve_seq, 1)
                dve.wait_ge(g1_ready, 2 * n + hf + 1)
                dve.wait_ge(dve_seq, seq + 1)
                dve.scalar_tensor_tensor(out=u1[:, hf, :], in0=u1[:, hf, :], scalar=1.0, in1=g1[:, hf, :],
                                         op0=ALU.add, op1=ALU.mult).then_inc(dve_seq, 1)
                dve.wait_ge(dve_seq, seq + 2)
                dve.wait_ge(s_ready, 2 * n + hf + 1)
                dve.tensor_tensor(a[:, 512 * hf:512 * hf + 512], u1[:, hf, :], sg[:, hf, :], ALU.mult).then_inc(a_ready, 1)

            LINKS = 5

            def pair(p, b, n, k, seq):
                onehots(p + 1, b, k + 1)
                iota = cm[:, bass.ds(C_IOTA + b * SLOT_TOKENS, SLOT_TOKENS)].unsqueeze(1).broadcast_to([P, 2, SLOT_TOKENS])
                dve.wait_ge(gt_done, n + 1)
                for t in range(TT):
                    ins = dve.tensor_tensor(
                        gsel[:, t, :].rearrange("p (e s) -> p e s", e=2), iota,
                        slot[:, t, bass.ds(2 * p, 2)].unsqueeze(2).broadcast_to([P, 2, SLOT_TOKENS]), ALU.is_equal)
                ins.then_inc(dve_seq, 1)
                dve.wait_ge(dve_seq, seq + 1)
                for t in range(TT):
                    v = gsel[:, t, :].rearrange("p (e s) -> p e s", e=2)
                    ins = dve.tensor_tensor(
                        v, v, gd[:, t, bass.ds(2 * p, 2)].unsqueeze(2).broadcast_to([P, 2, SLOT_TOKENS]), ALU.mult)
                ins.then_inc(gsel_ready, 1)
                swiglu(n, 0, seq + 1)
                add_out(0, k)
                add_out(1, k)
                swiglu(n, 1, seq + 3)
                add_out(2, k)
                add_out(3, k)
                bias_rows(p + 1)
                gathered(k + 1)
                dve.wait_ge(chunk_used, n * PAIR_CHUNKS + PAIR_CHUNKS)
                dve.tensor_copy(Y[:, 1, :], DN[1]).then_inc(y_ready, 1)

            def pairs(b, seq):
                n0, k0 = b * PAIRS, b * (PAIRS + 1)
                with dve.Fori(0, PAIRS) as p:
                    pair(p, b, n0 + p, k0 + p, seq + p * LINKS)
                dve.wait_ge(sc_free, 4 * (k0 + PAIRS) + 4)

            dve.sem_inc(sc_free, 4)
            onehots(0, 0, 0)
            x_lo(1)
            dve.wait_ge(e_ready, 1)
            link(dve.reciprocal(gst[:, :, 2], gst[:, :, 1]))
            link(dve.tensor_tensor(gate4[:, :, :], gate4[:, :, :], gst[:, :, 2:3].broadcast_to([P, TT, TOP_K]), ALU.mult))
            link(dve.tensor_tensor(hot[:, :, 1], hot[:, :, 0], gate4[:, :, :].unsqueeze(3).broadcast_to(every), ALU.mult))
            dve.tensor_reduce(gd[:, :, 0:N_EXPERTS], hot[:, :, 1].rearrange("p t j e -> p t e j"), AX_X,
                              ALU.add).then_inc(gd_ready, 1)
            dve.tensor_reduce(cnt[:, 0:1], m[:, 64:96], AX_X, ALU.max).then_inc(free_sem("ranks"), 1)
            gathered(0)
            bias_rows(0)
            dve.wait_ge(bguh_ready, 2)
            dve.tensor_tensor(bgul[:, :], bgu[:, :], bguh[:, :].bitcast(F32), ALU.subtract).then_inc(bgul_ready, 1)
            wait_read(dve, "ranks")
            dve.tensor_scalar(flag[0:1, 0:1], cnt[0:1, 0:1], float(SLOT_TOKENS), None, ALU.is_gt).then_inc(flag_ready, 1)
            dve.wait_ge(gd_ready, 1)
            seq0 = n_own[0]
            pairs(0, seq0)
            dve.wait_ge(flag_ready, 1)
            more = dve.value_load(flag[0:1, 0:1], min_val=0, max_val=1)
            with dve.If(more):
                with dve.Fori(1, PASSES) as b:
                    k0 = b * (PAIRS + 1)
                    for q in range(4):
                        add_out(q, b * (PAIRS + 1) - 1)
                    dve.memset(Y[:, :, :], 0.0)
                    dve.memset(gselT[:, :, :], 0.0).then_inc(zero_ready, 1)
                    onehots(0, b, k0)
                    bias_rows(0)
                    gathered(k0)
                    pairs(b, seq0 + b * (PAIRS * LINKS))
            for q in range(4):
                t, hf = q // 2, q % 2
                dve.wait_ge(last_done, q + 1)
                v = acc[:, t, 512 * hf:512 * hf + 512]
                dve.tensor_tensor(v, MISC[q], v, ALU.add).then_inc(all_done, 1)


_ORDER = ["x", "mem", "w_in", "w_mem_kv", "w_branch", "w_out", "g_mix", "g_mem", "g_ffn", "conv_w", "g_q_mem", "g_k_mem",
          "g_subln", "g_q_diff", "g_k_diff", "lambda_q1", "lambda_k1", "lambda_q2", "lambda_k2", "w_router", "b_router",
          "w_gate_up", "b_gate_up", "w_down", "b_down"]


def kernel(**inputs):
    import numpy as np
    import concourse.bacc as bacc
    from concourse.bass_utils import run_bass_kernel_spmd

    inv_freq = (1.0 / (np.float32(10000.0) ** (np.arange(0, 64, 2, dtype=np.float32) / np.float32(64)))).astype(np.float32)
    ang = np.arange(SEQ, dtype=np.float32)[:, None] * inv_freq[None, :]
    c_front = np.zeros((P, 256), np.float32)
    c_front[:, :P] = np.eye(P, dtype=np.float32)
    for t in range(TT):
        c_front[:, P + 64 * t:P + 64 * t + 32] = np.cos(ang[t * P:t * P + P])
        c_front[:, P + 64 * t + 32:P + 64 * t + 64] = np.sin(ang[t * P:t * P + P])
    c_moe = np.zeros((P, C_COLS), np.float32)
    row = np.arange(P, dtype=np.float32)
    c_moe[:, C_TRI:C_TRI + P] = row[:, None] < row[None, :]
    c_moe[:, C_IOTA:C_IOTA + SEQ] = np.arange(SEQ)
    c_moe[:, C_EROW:C_EROW + P] = (np.arange(P) // SLOT_TOKENS)[None, :]
    c_moe[:, C_PM:C_PM + PAIRS + 1] = row[:, None] - 2 * np.arange(PAIRS + 1)[None, :]
    c_moe[:, C_EIOTA:C_EIOTA + N_EXPERTS] = np.arange(N_EXPERTS)
    c_moe[:, C_ONES:C_ONES + P] = 1.0

    nc = bacc.Bacc("TRN2", target_bir_lowering=False, num_devices=1)
    arrays, args = {}, []
    for name, v in [(n, inputs[n]) for n in _ORDER] + [("c_front", c_front), ("c_moe", c_moe)]:
        v = np.ascontiguousarray(v)
        arrays[f"in_{name}"] = v
        args.append(nc.dram_tensor(f"in_{name}", v.shape, mybir.dt.from_np(v.dtype), kind="ExternalInput").ap())
    args.append(nc.dram_tensor("out_0", (1, SEQ, D), F32, kind="ExternalOutput").ap())
    build(nc, *args)
    r = run_bass_kernel_spmd(nc, [arrays], core_ids=[0])
    return r.results[0]["out_0"]
```

```python
from contextlib import ExitStack

import concourse.bass as bass
from concourse import mybir

ALU = mybir.AluOpType
ACT = mybir.ActivationFunctionType
F32 = mybir.dt.float32
F32R = mybir.dt.float32r
I32 = mybir.dt.int32
U32 = mybir.dt.uint32
BF16 = mybir.dt.bfloat16
AX_X = mybir.AxisListType.X

P = 128
D = 1024
SEQ = 256
TT = SEQ // P
KD = D // P
EPS = 1e-6
LAM_INIT = 0.2
SWIGLU_LIMIT = 7.0
SWIGLU_ALPHA = 1.702
NEG = -1e30
N_EXPERTS = 32
TOP_K = 4
PAIRS = N_EXPERTS // 2
SLOT_TOKENS = 64
PASSES = SEQ // SLOT_TOKENS

SLOTS = 12
SLOT_W = 2048
FRONT_UNITS = 40
HALVES = 2 * FRONT_UNITS
W_BUFS = 3
EXTRA = 4
PAIR_CHUNKS = 24

V_MEM, V_MIX, V_FFN, V_CONV, V_GQM, V_GKM, V_SUB, V_ROWS = 0, 8, 16, 24, 36, 37, 38, 39

C_TRI, C_IOTA, C_EROW, C_PM, C_EIOTA, C_ONES = 0, 128, 384, 512, 530, 562
C_COLS = 704


TASKS = ["vecm", "memT0", "memT1", "vec", "xT0", "xT1", "mkT", "mqT", "ms0", "ms1", "mp0", "mav0", "mp1", "mav1", "dqT", "dkT",
         "ds00", "ds01", "da0", "ds10", "dav0", "ds11", "da1", "dav1", "dy0", "dy1", "XT0", "XT1", "XT2", "XT3", "ranks"]


def front_units():
    units = []
    for name in ("mk", "mv", "mq", "dq", "dk", "dv", "cc", "ch", "cb"):
        units += [(name, 0), (name, 1)]
    for i in (2, 1, 0):
        for half in range(2):
            units += [(f"gate{i}", 2 * half), (f"gate{i}", 2 * half + 1), (f"branch{i}", half)]
    units += [("out", n) for n in range(4)]
    return units


def build(nc, x, mem, w_in, w_mem_kv, w_branch, w_out, g_mix, g_mem, g_ffn, conv_w, g_q_mem, g_k_mem,
          g_subln, g_q_diff, g_k_diff, lambda_q1, lambda_k1, lambda_q2, lambda_k2, w_router, b_router,
          w_gate_up, b_gate_up, w_down, b_down, c_front, c_moe, out):
    units = front_units()
    assert len(units) == FRONT_UNITS

    use_of, last_of = [], {}
    n_use = -1
    for h in range(HALVES):
        name = units[h // 2][0]
        if h % 2 == 0 or name.startswith("branch"):
            n_use += 1
        use_of.append(n_use)
        last_of[n_use] = h
    N_USES = n_use + 1

    with ExitStack() as ctx:
        def sem(name):
            return ctx.enter_context(nc.semaphore(name))

        def sb(stack, name, shape, dt=F32):
            return stack.enter_context(nc.sbuf_tensor(name, shape, dt))

        ring = sb(ctx, "ring", [P, SLOTS, SLOT_W])
        acc = sb(ctx, "acc", [P, TT, D])
        ident = sb(ctx, "ident", [P, 256])
        vecT = sb(ctx, "vecT", [P, V_ROWS])
        stat = sb(ctx, "stat", [P, 3, 62])
        att = sb(ctx, "att", [P, 4, 24])
        lam = sb(ctx, "lam", [P, 8])
        flag = sb(ctx, "flag", [1, 1], I32)
        x1sq = sb(ctx, "x1sq", [P, TT, 4])

        with ExitStack() as front:
            with ExitStack() as conv:
                u = sb(conv, "u", [P, 4, 256])
                cb = sb(conv, "cb", [P, 4, 256])
            ych = sb(front, "ych", [P, 4, 256], F32R)
            ycl = sb(front, "ycl", [P, 4, 256], F32R)
            PT = sb(front, "PT", [P, 1024])
            S = sb(front, "S", [P, 2, 1024])
            T = sb(front, "T", [P, 2, 1024])
            R = sb(front, "R", [P, 4, 1024])
            WH = sb(front, "WH", [P, W_BUFS, 4, 256], F32R)
            WL = sb(front, "WL", [P, W_BUFS, 4, 256], F32R)
            hTh = sb(front, "hTh", [P, KD, SEQ], F32R)
            hTl = sb(front, "hTl", [P, KD, SEQ], F32R)
            mTh = sb(front, "mTh", [P, KD, SEQ], F32R)
            mTl = sb(front, "mTl", [P, KD, SEQ], F32R)
            gqk = sb(front, "gqk", [P, 2, 64])

        extra = []
        with ExitStack() as moe:
            bgu = sb(moe, "bgu", [P, 2 * D])
            cm = sb(moe, "cm", [P, C_COLS])
            wr = sb(moe, "wr", [P, KD, N_EXPERTS])
            br = sb(moe, "br", [P, N_EXPERTS])
            sb(moe, "over_PT", [P, 1024 - C_COLS - KD * N_EXPERTS - N_EXPERTS])
            Y = sb(moe, "Y", [P, 2, 512])
            a = sb(moe, "a", [P, D])
            bguh = sb(moe, "bguh", [P, 2 * D], F32R)
            bgul = sb(moe, "bgul", [P, 2 * D], F32R)
            X = sb(moe, "X", [P, TT, D])
            with ExitStack() as early:
                extra += [sb(early, f"extra{i}", [P, SLOT_W]) for i in range(2)]
            g1 = sb(moe, "g1", [P, 2, 512])
            u1 = sb(moe, "u1", [P, 2, 512])
            sg = sb(moe, "sg", [P, 2, 512])
            sb(moe, "over_W", [P, D])
            xg = sb(moe, "xg", [P, KD, P])
            aT = sb(moe, "aT", [P, KD, P])
            extra += [sb(moe, f"extra{i}", [P, SLOT_W]) for i in range(2, EXTRA)]
            hT2 = sb(moe, "hT2", [P, KD, SEQ])
            lg = sb(moe, "lg", [P, TT, N_EXPERTS])
            top = sb(moe, "top", [P, TT, 8])
            topi = sb(moe, "topi", [P, TT, 8], U32)
            topf = sb(moe, "topf", [P, TT, 8])
            gate4 = sb(moe, "gate4", [P, TT, TOP_K])
            gst = sb(moe, "gst", [P, TT, 4])
            hot = sb(moe, "hot", [P, TT, 2, TOP_K, N_EXPERTS])
            msk = sb(moe, "msk", [P, TT, N_EXPERTS], BF16)
            cmb = sb(moe, "cmb", [P, 2, P], BF16)
            gd = sb(moe, "gd", [P, TT, P])
            slot = sb(moe, "slot", [P, TT, N_EXPERTS + 2])
            cnt = sb(moe, "cnt", [P, 2])
            oh = sb(moe, "oh", [P, P], F32R)
            sel = sb(moe, "sel", [P, TT, P])
            gsel = sb(moe, "gsel", [P, TT, P])
            gselT = sb(moe, "gselT", [P, TT, P])

        U = [ctx.enter_context(nc.psum_tensor(f"U{i}", [P, 512], F32)) for i in range(4)]
        M = [ctx.enter_context(nc.psum_tensor(f"M{i}", [P, 1024], F32)) for i in range(2)]

        half_in = sem("half_in")
        landed = [sem(f"landed{i}") for i in range(SLOTS)]
        mem_in = [sem(f"mem_in{t}") for t in range(TT)]
        x_in, id_in, gmem_in, row_in, vec_in, lam_in, gqk_in, wr_in, cm_in, bgu_in, bdn_in, out_done = (sem(n) for n in (
            "x_in", "id_in", "gmem_in", "row_in", "vec_in", "lam_in", "gqk_in", "wr_in", "cm_in", "bgu_in", "bdn_in",
            "out_done"))
        wh_ready = sem("wh_ready")
        w_ready = sem("w_ready")
        w_used = sem("w_used")
        u_free = [sem(f"u_free{i}") for i in range(4)]
        m_full = [sem(f"m_full{i}") for i in range(2)]
        m_free = [sem(f"m_free{i}") for i in range(2)]
        dve_seq, act_seq = sem("dve_seq"), sem("act_seq")
        eps_ready, ss_ready, sd_ready, sq_ready = (sem(n) for n in ("eps_ready", "ss_ready", "sd_ready", "sq_ready"))
        mem_rstd_ready, xn_ready, hi_ready = sem("mem_rstd_ready"), sem("xn_ready"), sem("hi_ready")
        heads_ready = sem("heads_ready")
        nmx_ready, p_ready, pn_ready = sem("nmx_ready"), sem("p_ready"), sem("pn_ready")
        ydiff_ready, yconv_ready = sem("ydiff_ready"), sem("yconv_ready")
        lam_sum, lam_exp, lam_ready = sem("lam_sum"), sem("lam_exp"), sem("lam_ready")
        conv_ready, ych_ready = sem("conv_ready"), sem("ych_ready")
        merged_ready, mh_ready, ml_ready = (sem(n) for n in ("merged_ready", "mh_ready", "ml_ready"))
        x1sq_ready, cmb_ready, logits_done, rstd_ready = (
            sem(n) for n in ("x1sq_ready", "cmb_ready", "logits_done", "rstd_ready"))
        pad_ready = sem("pad_ready")
        X_ready = sem("X_ready")
        top_ready, e_ready, msk_ready, gd_ready, flag_ready = (
            sem(n) for n in ("top_ready", "e_ready", "msk_ready", "gd_ready", "flag_ready"))
        bguh_ready, bgul_ready = sem("bguh_ready"), sem("bgul_ready")
        extra_in = [sem(f"extra_in{i}") for i in range(EXTRA)]
        chunk_used = sem("chunk_used")
        sel_ready, oh_ready, gsel_ready, gather_done, xg_ready = (
            sem(n) for n in ("sel_ready", "oh_ready", "gsel_ready", "gather_done", "xg_ready"))
        gu_done, g1_ready, s_ready, a_ready = (sem(n) for n in ("gu_done", "g1_ready", "s_ready", "a_ready"))
        gt_done, gt_ready, at_done, at_ready = (sem(n) for n in ("gt_done", "gt_ready", "at_done", "at_ready"))
        y_ready, sc_done, sc_free, zero_ready = (sem(n) for n in ("y_ready", "sc_done", "sc_free", "zero_ready"))
        dn_done = sem("dn_done")
        last_done, all_done = sem("last_done"), sem("all_done")

        def wait_full(eng, task):
            j = TASKS.index(task)
            eng.wait_ge(m_full[j % 2], j // 2 + 1)

        def wait_read(eng, task):
            j = TASKS.index(task)
            eng.wait_ge(m_free[j % 2], j // 2 + 1)

        def misc(task):
            return M[TASKS.index(task) % 2]

        def free_sem(task):
            return m_free[TASKS.index(task) % 2]

        DN = [M[1][:, 0:512], M[1][:, 512:1024]]
        C = [M[0][:, 0:512], M[0][:, 512:1024]]
        MISC = [DN[0], DN[1], C[0], C[1]]
        LOGITS = C[1][:, 0:TT * N_EXPERTS]

        def idm():
            return ident[:, 0:P]

        def unit_src(c):
            name, part = units[c]
            if name in ("mk", "mv"):
                col = {"mk": 0, "mv": 512}[name] + 256 * part
                return w_mem_kv[0].rearrange("(k p) n -> p k n", p=P)[:, :, col:col + 256]
            if name.startswith("branch"):
                return w_branch[0, int(name[-1])].rearrange("(k p) n -> p k n", p=P)[:, :, 512 * part:512 * part + 512]
            if name == "out":
                return w_out[0].rearrange("(k p) n -> p k n", p=P)[:, :, 256 * part:256 * part + 256]
            if name.startswith("gate"):
                col = 3584 + 1024 * int(name[-1]) + 256 * part
            else:
                col = {"dq": 0, "dk": 512, "dv": 1024, "cb": 1536, "cc": 2048, "ch": 2560, "mq": 3072}[name] + 256 * part
            return w_in[0].rearrange("(k p) n -> p k n", p=P)[:, :, col:col + 256]

        def half_src(h):
            c, j = divmod(h, 2)
            s = ring[:, c % SLOTS, :]
            if units[c][0].startswith("branch"):
                return s.rearrange("p (k n) -> p k n", k=4)[:, :, 256 * j:256 * j + 256]
            return s.rearrange("p (k n) -> p k n", k=8)[:, 4 * j:4 * j + 4, :]

        def raw(i):
            return R[:, i, :].rearrange("p (t n) -> p t n", t=TT)

        PAIR_START = FRONT_UNITS + PAIR_CHUNKS - EXTRA
        assert PAIR_CHUNKS % SLOTS == 0

        def is_extra(first, i):
            return first and SLOTS <= i < SLOTS + EXTRA

        def place(first, i):
            return PAIR_START + i if not first else FRONT_UNITS + i - (EXTRA if i >= SLOTS else 0)

        def chunk_sem(first, i):
            return extra_in[i - SLOTS] if is_extra(first, i) else landed[place(first, i) % SLOTS]

        def wait_chunk(eng, n, i, first):
            if is_extra(first, i):
                eng.wait_ge(extra_in[i - SLOTS], 16)
            elif first:
                eng.wait_ge(chunk_sem(first, i), 16 * (place(first, i) // SLOTS + 1))
            else:
                eng.wait_ge(chunk_sem(first, i),
                            n * (16 * PAIR_CHUNKS // SLOTS) + 16 * ((place(first, i) - PAIR_CHUNKS) // SLOTS + 1))

        def pair_chunk(i, first):
            if is_extra(first, i):
                s = extra[i - SLOTS][:, :]
            else:
                s = ring[:, place(first, i) % SLOTS, :]
            return s if i < 16 else s.rearrange("p (f n) -> p f n", f=2)

        def wait_product(eng, use):
            eng.wait_ge(w_used, last_of[use] + 1)

        def wait_unit(eng, c):
            eng.wait_ge(u_free[use_of[2 * c] % 4], use_of[2 * c] // 4 + 1)

        def merged(i):
            return R[:, i // 2, (i % 2) * 512:(i % 2) * 512 + 512].rearrange("p (s n) -> p s n", s=2)

        def gates(i):
            return T[:, 0, (i % 2) * 512:(i % 2) * 512 + 512].rearrange("p (s n) -> p s n", s=2)

        def first_unit(name):
            return [n for n, _ in units].index(name)

        def merge_order(name):
            return (first_unit("branch" + name[-1]) - first_unit("branch2")) // 6

        def scratch2(i):
            return S[:, 0, (i % 2) * 512:(i % 2) * 512 + 512].rearrange("p (s n) -> p s n", s=2)

        def bank2(m):
            return m[:, :].rearrange("p (k n) -> p k n", k=4)

        RAW_OF = {"mk": 0, "mv": 1, "mq": 2, "dq": 3, "dk": 0, "dv": 2}
        ST = {"mem": (0, 2), "x": (2, 2), "mk": (4, 8), "mq": (12, 8), "dq": (20, 16), "dk": (36, 16),
              "y0": (52, 4), "y1": (56, 4), "x1": (60, 2)}
        MEM_SCALE, DIFF_SCALE = 128.0 ** -0.5, 64.0 ** -0.5

        block = ctx.enter_context(nc.Block())

        @block.sync
        def _(sp):
            sp.dma_start(ident[:, :], c_front[:, :]).then_inc(id_in, 16)
            for t in range(TT):
                sp.dma_start(S[:, t, :], mem[0, t * P:t * P + P, :]).then_inc(mem_in[t], 16)
            for c in range(FRONT_UNITS):
                if c >= SLOTS:
                    sp.wait_ge(w_ready, 2 * (c - SLOTS) + 2)
                name = units[c][0]
                k = 4 if name.startswith("branch") else 8
                dst = ring[:, c % SLOTS, :].rearrange("p (k n) -> p k n", k=k)
                if c == 0:
                    sp.dma_start(dst[:, 0:4], unit_src(c)[:, 0:4]).then_inc(half_in, 16)
                    sp.dma_start(dst[:, 4:8], unit_src(c)[:, 4:8]).then_inc(landed[c], 16)
                else:
                    sp.dma_start(dst, unit_src(c)).then_inc(landed[c % SLOTS], 16)
                if c == 1:
                    sp.dma_start(acc[:, :, :], x[0].rearrange("(t p) d -> p t d", p=P)).then_inc(x_in, 16)

            gu = w_gate_up[0].rearrange("e (k p) f -> e p k f", p=P)
            dn = w_down[0].rearrange("e (k p) d -> e p k d", p=P)

            def load(e0, i, first=False):
                k, e = divmod(i % 16, 2)
                if i < 16:
                    src = gu[bass.ds(e0 + e, 1), :, k, :].rearrange("a p f -> p (a f)")
                else:
                    src = dn[bass.ds(e0 + e, 1), :, 2 * k:2 * k + 2, :].rearrange("a p k d -> p (a k) d")
                sp.dma_start(pair_chunk(i, first), src).then_inc(chunk_sem(first, i), 16)

            for i in range(PAIR_CHUNKS):
                if i < SLOTS:
                    sp.wait_ge(w_ready, 2 * (FRONT_UNITS + i - SLOTS) + 2)
                elif is_extra(True, i):
                    sp.wait_ge(w_used, HALVES)
                else:
                    sp.wait_ge(chunk_used, i - EXTRA - SLOTS + 1)
                load(0, i, first=True)
            for i in range(PAIR_CHUNKS):
                sp.wait_ge(chunk_used, PAIR_CHUNKS + i - SLOTS + 1 - (EXTRA if i < EXTRA else 0))
                load(2, i)
            with sp.Fori(2, PAIRS) as n:
                for i in range(PAIR_CHUNKS):
                    sp.wait_ge(chunk_used, n * PAIR_CHUNKS + (i - SLOTS + 1))
                    load(2 * n, i)
            sp.wait_ge(flag_ready, 1)
            more = sp.value_load(flag[0:1, 0:1], min_val=0, max_val=1)
            with sp.If(more):
                with sp.Fori(1, PASSES) as b:
                    with sp.Fori(0, PAIRS) as n:
                        for i in range(PAIR_CHUNKS):
                            sp.wait_ge(chunk_used, b * (PAIRS * PAIR_CHUNKS) + n * PAIR_CHUNKS + (i - SLOTS + 1))
                            load(2 * n, i)
            for q in range(4):
                t, hf = q // 2, q % 2
                sp.wait_ge(all_done, q + 1)
                sp.dma_start(out[0, t * P:t * P + P, hf * 512:hf * 512 + 512],
                             acc[:, t, hf * 512:hf * 512 + 512]).then_inc(out_done, 16)
            sp.wait_ge(out_done, 4 * 16)

        @block.gpsimd
        def _(pool):
            for at, v in ((V_GQM, g_q_mem), (V_GKM, g_k_mem), (V_SUB, g_subln)):
                pool.dma_start(PT[at:at + 1, 0:P], v).then_inc(row_in, 16)
            pool.dma_start(PT[V_CONV:V_CONV + 12, 0:P],
                           conv_w[0].rearrange("j (k p) -> (j k) p", p=P)).then_inc(row_in, 16)
            for i, v in enumerate((lambda_q1, lambda_k1, lambda_q2, lambda_k2)):
                pool.dma_start(PT[:, 256 + 64 * i:320 + 64 * i], v.broadcast_to([P, 64])).then_inc(lam_in, 16)
            for i, v in enumerate((g_q_diff, g_k_diff)):
                pool.dma_start(gqk[:, i, :], v.broadcast_to([P, 64])).then_inc(gqk_in, 16)
            pool.wait_ge(w_used, 2 * first_unit("branch1") + 8)
            nc.gpsimd.memset(bgu[:, :], 0.0).then_inc(pad_ready, 1)
            wait_read(pool, "dav1")
            pool.dma_start(cm[:, :], c_moe[:, :]).then_inc(cm_in, 16)
            pool.dma_start(wr[:, :, :], w_router[0].rearrange("(k p) e -> p k e", p=P)).then_inc(wr_in, 16)
            pool.dma_start(br[:, :], b_router.broadcast_to([P, N_EXPERTS])).then_inc(wr_in, 16)
            pool.wait_ge(pad_ready, 1)
            pool.dma_start(bgu[0:N_EXPERTS, :], b_gate_up[0]).then_inc(bgu_in, 16)
            pool.wait_ge(merged_ready, 12)
            nc.gpsimd.memset(Y[:, :, :], 0.0).then_inc(pad_ready, 1)
            pool.wait_ge(pad_ready, 2)
            pool.dma_start(Y[0:N_EXPERTS, :, :], b_down[0].rearrange("e (h n) -> e h n", h=2)).then_inc(bdn_in, 16)

        @block.tensor
        def _(pe):
            n_begun = [0]

            def begin(task):
                j = TASKS.index(task)
                assert j == n_begun[0]
                n_begun[0] += 1
                if j >= 2:
                    pe.wait_ge(m_free[j % 2], j // 2)
                return M[j % 2]

            def end(task, mm):
                mm.then_inc(m_full[TASKS.index(task) % 2], 1)

            def transpose_act(task, src, k0):
                m = bank2(begin(task))
                for k in range(4):
                    for t in range(TT):
                        mm = pe.transpose(m[:, k, t * P:t * P + P], src[:, t, (k0 + k) * P:(k0 + k + 1) * P], idm())
                end(task, mm)

            def transpose_heads(task, i):
                m = bank2(begin(task))
                for h in range(4):
                    for t in range(TT):
                        mm = pe.transpose(m[:, h, t * P:t * P + P], raw(i)[:, t, h * P:h * P + P], idm())
                end(task, mm)

            def mem_scores(t):
                task = f"ms{t}"
                m = bank2(begin(task))
                for h in range(4):
                    mm = pe.matmul(m[:, h, :], T[:, 1, h * 256 + t * P:h * 256 + t * P + P],
                                   T[:, 0, h * 256:h * 256 + 256], start=True, stop=True)
                end(task, mm)

            def mem_pT(t):
                pe.wait_ge(pn_ready, t + 1)
                m = begin(f"mp{t}")
                for h in range(4):
                    for mt in range(2):
                        mm = pe.transpose(m[:, (2 * h + mt) * P:(2 * h + mt + 1) * P],
                                          S[:, t, h * 256 + mt * P:h * 256 + mt * P + P], idm())
                end(f"mp{t}", mm)

            def mem_av(t):
                wait_read(pe, f"mp{t}")
                for c in range(2):
                    wait_unit(pe, first_unit("mv") + c)
                m = begin(f"mav{t}")
                for h in range(4):
                    for mt in range(2):
                        mm = pe.matmul(m[:, h * P:h * P + P], raw(1)[:, mt, h * P:h * P + P],
                                       PT[:, (2 * h + mt) * P:(2 * h + mt + 1) * P], start=(mt == 0), stop=(mt == 1))
                end(f"mav{t}", mm)

            def diff_scores(t, hp):
                task = f"ds{t}{hp}"
                m = bank2(begin(task))
                for hh in range(2):
                    for c in range(2):
                        h = 2 * hp + hh
                        mm = pe.matmul(m[:, 2 * c + hh, 0:P * (t + 1)],
                                       T[64 * c:64 * c + 64, 1, h * 256 + t * P:h * 256 + t * P + P],
                                       T[64 * c:64 * c + 64, 0, h * 256:h * 256 + P * (t + 1)], start=True, stop=True)
                end(task, mm)

            def diff_aT(t):
                pe.wait_ge(pn_ready, 2 + 2 * t + 2)
                m = begin(f"da{t}")
                for h in range(4):
                    for kt in range(t + 1):
                        i = h * (t + 1) + kt
                        mm = pe.transpose(m[:, i * P:i * P + P],
                                          S[:, h // 2, (h % 2) * 256 + kt * P:(h % 2) * 256 + kt * P + P], idm())
                end(f"da{t}", mm)

            def diff_av(t):
                wait_read(pe, f"da{t}")
                for c in range(2):
                    wait_unit(pe, first_unit("dv") + c)
                m = begin(f"dav{t}")
                for h in range(4):
                    for kt in range(t + 1):
                        i = h * (t + 1) + kt
                        mm = pe.matmul(m[:, h * P:h * P + P], PT[:, i * P:i * P + P],
                                       raw(2)[:, kt, h * P:h * P + P], start=(kt == 0), stop=(kt == t))
                end(f"dav{t}", mm)

            def diff_yT(t):
                pe.wait_ge(ydiff_ready, t + 1)
                m = begin(f"dy{t}")
                for h in range(4):
                    mm = pe.transpose(m[:, h * P:h * P + P], raw(3)[:, t, h * P:h * P + P], idm())
                end(f"dy{t}", mm)

            def half_unit(h):
                c, j = divmod(h, 2)
                name, part = units[c]
                use = use_of[h]
                whole = name.startswith("branch")
                begins, ends = whole or j == 0, whole or j == 1
                bank = U[use % 4][:, :].rearrange("p (s n) -> p s n", s=2)
                if begins and use >= 4:
                    pe.wait_ge(u_free[use % 4], use // 4)
                starts = name == "mk" and part == 0
                if starts:
                    pe.wait_ge(hi_ready, j + 1)
                if part == 0 and j == 0:
                    if name == "mq":
                        wait_read(pe, "xT0")
                        wait_read(pe, "xT1")
                    if name == "branch2":
                        wait_read(pe, "mav0")
                        wait_read(pe, "mav1")
                    if name == "branch1":
                        pe.wait_ge(yconv_ready, 4)
                    if name == "branch0":
                        wait_read(pe, "dy0")
                        wait_read(pe, "dy1")
                pe.wait_ge(w_ready, h + 1)
                k0 = 4 * j
                if name in ("mk", "mv"):
                    ah, al = mTh, mTl
                elif name == "branch1":
                    ah, al, k0 = ych, ycl, 0
                elif name == "branch2":
                    ah, al, k0 = mTh, mTl, 0
                elif name == "branch0":
                    ah, al, k0 = mTh, mTl, 4
                else:
                    ah, al = hTh, hTl
                w_hi, w_lo = WH[:, h % W_BUFS], WL[:, h % W_BUFS]
                tokens_out = name in ("mk", "mv", "mq", "dq", "dk", "dv", "out")
                passes = ((ah, w_hi), (ah, w_lo), (al, w_hi))
                order = [(k, s, q) for k in range(4) for s in range(2) for q in range(3)]
                if starts:
                    order.sort(key=lambda step: step[2])
                for n, (k, s, q) in enumerate(order):
                    if name == "out" and part == 0 and n in (0, 12):
                        pe.wait_ge(ml_ready, 2 * j + n // 12 + 1)
                    if starts and n == 16:
                        wait_read(pe, f"memT{j}")
                    aa, ww = passes[q]
                    if tokens_out:
                        lhsT, rhs = aa[:, k0 + k, s * P:s * P + P], ww[:, k, :]
                    else:
                        lhsT, rhs = ww[:, k, s * P:s * P + P], aa[:, k0 + k, :]
                    mm = pe.matmul(bank[:, s, :], lhsT, rhs, start=begins and n == 0, stop=ends and n == 23,
                                   skip_group_check=True)
                mm.then_inc(w_used, 1)

            def x1_transposes(n):
                wait_unit(pe, first_unit("out") + n)
                m = begin(f"XT{n}")
                for k in range(2):
                    for t in range(TT):
                        mm = pe.transpose(m[:, (2 * k + t) * P:(2 * k + t) * P + P],
                                          acc[:, t, (2 * n + k) * P:(2 * n + k + 1) * P], idm())
                end(f"XT{n}", mm)

            def logits(n):
                wait_read(pe, f"XT{n}")
                if n == 0:
                    pe.wait_ge(wr_in, 32)
                    wait_read(pe, "dy0")
                for k in (2 * n, 2 * n + 1):
                    for t in range(TT):
                        mm = pe.matmul(LOGITS[:, t * N_EXPERTS:(t + 1) * N_EXPERTS], hT2[:, k, t * P:t * P + P],
                                       wr[:, k, :], start=(k == 0 and t == 0), stop=(k == KD - 1 and t == 1),
                                       skip_group_check=True)
                if n == 3:
                    mm.then_inc(logits_done, 1)

            def bias_half(hf):
                for nb in (hf, 2 + hf):
                    for q, bb in enumerate((bguh, bgul)):
                        pe.matmul(U[nb][:, :], oh[:, :], bb[:, nb * 512:nb * 512 + 512],
                                  start=(q == 0), stop=False, skip_group_check=True)

            pe.wait_ge(id_in, 16)
            pe.wait_ge(gmem_in, 16)
            m = begin("vecm")
            end("vecm", pe.transpose(m[:, 0:8], PT[0:8, 0:P], ident[0:8, 0:8]))
            for t in range(TT):
                pe.wait_ge(mem_in[t], 16)
            transpose_act("memT0", S, 0)
            transpose_act("memT1", S, 4)
            for h in range(HALVES):
                half_unit(h)
                if h == 0:
                    pe.wait_ge(vec_in, 16 * 2)
                    pe.wait_ge(row_in, 16 * 4)
                    m = begin("vec")
                    end("vec", pe.transpose(m[:, 0:V_ROWS], PT[0:V_ROWS, 0:P], ident[0:V_ROWS, 0:V_ROWS]))
                if h == 3:
                    pe.wait_ge(xn_ready, 2)
                    transpose_act("xT0", R[:, 2:4, :], 0)
                    transpose_act("xT1", R[:, 2:4, :], 4)
                if h == 9:
                    pe.wait_ge(heads_ready, 1)
                    transpose_heads("mkT", 0)
                if h == 16:
                    pe.wait_ge(heads_ready, 2)
                    transpose_heads("mqT", 2)
                if h == 18:
                    wait_read(pe, "mkT")
                    wait_read(pe, "mqT")
                    mem_scores(0)
                    mem_scores(1)
                if h == 21:
                    mem_pT(0)
                if h == 23:
                    mem_av(0)
                    mem_pT(1)
                if h == 25:
                    mem_av(1)
                if h == 27:
                    pe.wait_ge(heads_ready, 3)
                    transpose_heads("dqT", 3)
                if h == 29:
                    pe.wait_ge(heads_ready, 4)
                    transpose_heads("dkT", 0)
                if h == 31:
                    wait_read(pe, "dqT")
                    wait_read(pe, "dkT")
                    diff_scores(0, 0)
                    diff_scores(0, 1)
                if h == 36:
                    diff_aT(0)
                    diff_scores(1, 0)
                if h == 38:
                    diff_av(0)
                if h == 39:
                    diff_scores(1, 1)
                if h == 43:
                    diff_aT(1)
                if h == 45:
                    diff_av(1)
                if h == 47:
                    diff_yT(0)
                if h == 52:
                    diff_yT(1)
                if h == 75:
                    x1_transposes(0)
                if h == 77:
                    x1_transposes(1)
                if h == 78:
                    logits(0)

            x1_transposes(2)
            logits(1)
            x1_transposes(3)
            logits(2)
            logits(3)
            for q in range(4):
                pe.wait_ge(u_free[(N_USES - 4 + q) % 4], (N_USES - 4 + q) // 4 + 1)
            pe.wait_ge(oh_ready, 1)
            pe.wait_ge(bgul_ready, 2)
            bias_half(0)
            pe.wait_ge(cmb_ready, 1)
            pe.wait_ge(msk_ready, 1)
            tri, ones = cmb[:, 0, :], cmb[:, 1, :]
            m = begin("ranks")
            pe.matmul(m[:, 0:32], tri, msk[:, 0, :], start=True, stop=True)
            pe.matmul(m[:, 32:64], ones, msk[:, 0, :], start=True, stop=False)
            pe.matmul(m[:, 32:64], tri, msk[:, 1, :], start=False, stop=True)
            pe.matmul(m[:, 64:96], ones, msk[:, 0, :], start=True, stop=False)
            end("ranks", pe.matmul(m[:, 64:96], ones, msk[:, 1, :], start=False, stop=True))

            def gather(k):
                pe.wait_ge(sel_ready, k + 1)
                for dh in range(2):
                    for dd in range(4):
                        d = 4 * dh + dd
                        for t in range(TT):
                            mm = pe.matmul(DN[dh][:, dd * P:dd * P + P], X[:, t, d * P:d * P + P], sel[:, t, :],
                                           start=(t == 0), stop=(t == 1))
                    mm.then_inc(gather_done, 1)

            def scatter(signal):
                for q in range(4):
                    t, hf = q // 2, q % 2
                    pe.matmul(MISC[q], gselT[:, t, :], Y[:, hf, :], start=True, stop=True).then_inc(signal, 1)

            def down(n, kk, first):
                pe.wait_ge(at_ready, 2 * n + 1 + kk // 2)
                for experts in ((0,), (1,)) if kk == 3 else ((0, 1),):
                    for e in experts:
                        i = 16 + 2 * kk + e
                        wait_chunk(pe, n, i, first)
                    for hf in range(2):
                        for f2 in range(2):
                            f = 2 * kk + f2
                            for e in experts:
                                mm = pe.matmul(DN[hf][64 * e:64 * e + 64, :], aT[:, f, 64 * e:64 * e + 64],
                                               pair_chunk(16 + 2 * kk + e, first)[:, f2, hf * 512:hf * 512 + 512],
                                               start=(f == 0), stop=(f == KD - 1), skip_group_check=True)
                                if f2 == 1 and hf == 1:
                                    mm.then_inc(chunk_used, 1)
                                elif f2 == 1 and kk == 3 and e == 1:
                                    mm.then_inc(dn_done, 1)

            def pair(n, k, first=False):
                if not first:
                    pe.wait_ge(oh_ready, k + 1)
                    bias_half(0)
                    bias_half(1)
                pe.wait_ge(xg_ready, 2 * k + 2)
                for kk in range(KD):
                    if kk == 2:
                        pe.wait_ge(y_ready, 2 * n + 2)
                        pe.wait_ge(gt_ready, n + 1)
                        scatter(sc_done)
                    if kk == 6:
                        pe.wait_ge(gsel_ready, n + 1)
                        pe.wait_ge(sc_free, 4 * k + 4 + 4)
                        pe.transpose(C[0][:, 0:P], gsel[:, 0, :], idm())
                        pe.transpose(C[0][:, P:2 * P], gsel[:, 1, :], idm()).then_inc(gt_done, 1)
                    for e in range(2):
                        i = 2 * kk + e
                        wait_chunk(pe, n, i, first)
                    for nb in (0, 2, 1, 3):
                        for e in range(2):
                            mm = pe.matmul(U[nb][64 * e:64 * e + 64, :], xg[:, kk, 64 * e:64 * e + 64],
                                           pair_chunk(2 * kk + e, first)[:, nb * 512:nb * 512 + 512],
                                           start=False, stop=(kk == KD - 1), skip_group_check=True)
                            if nb == 3:
                                mm.then_inc(chunk_used, 1)
                            elif nb == 2 and kk == KD - 1 and e == 1:
                                mm.then_inc(gu_done, 1)
                gather(k + 1)
                for hf in range(2):
                    pe.wait_ge(a_ready, 2 * n + hf + 1)
                    if hf == 1:
                        pe.wait_ge(gt_ready, n + 2)
                    for f in range(4):
                        mm = pe.transpose(C[1 - hf][:, f * P:f * P + P], a[:, (4 * hf + f) * P:(4 * hf + f + 1) * P], idm())
                    mm.then_inc(at_done, 1)
                    if hf == 0:
                        pe.wait_ge(xg_ready, 2 * k + 4)
                        down(n, 0, first)
                for kk in range(1, 4):
                    down(n, kk, first)

            def pairs(n0, k0, begin=0):
                with pe.Fori(begin, PAIRS) as p:
                    pair(n0 + p, k0 + p)
                pe.wait_ge(y_ready, n0 * 2 + (2 * PAIRS + 2))
                pe.wait_ge(gt_ready, n0 + (PAIRS + 1))

            bias_half(1)
            pe.wait_ge(X_ready, 2)
            gather(0)
            pe.wait_ge(gd_ready, 1)
            wait_read(pe, "ranks")
            pe.transpose(C[0][:, 0:P], gd[:, 0, :], idm())
            pe.transpose(C[0][:, P:2 * P], gd[:, 1, :], idm()).then_inc(gt_done, 1)
            pe.wait_ge(bdn_in, 16)
            pe.wait_ge(flag_ready, 1)
            more = pe.value_load(flag[0:1, 0:1], min_val=0, max_val=1)
            pair(0, 0, first=True)
            pairs(0, 0, begin=1)
            with pe.If(more):
                with pe.Fori(1, PASSES) as b:
                    scatter(sc_done)
                    pe.wait_ge(sc_free, b * (PAIRS + 1) * 4 + 4)
                    pe.wait_ge(zero_ready, b)
                    gather(b * (PAIRS + 1))
                    pairs(b * PAIRS, b * (PAIRS + 1))
            scatter(last_done)

        @block.scalar
        def _(act):
            n_own = [0]

            def link(ins):
                n_own[0] += 1
                ins.then_inc(act_seq, 1)
                act.wait_ge(act_seq, n_own[0])

            def split_hi(h):
                if h >= W_BUFS:
                    act.wait_ge(w_used, h - W_BUFS + 1)
                if h == 0:
                    act.wait_ge(half_in, 16)
                else:
                    act.wait_ge(landed[(h // 2) % SLOTS], 16 * (h // 2 // SLOTS + 1))
                act.copy(WH[:, h % W_BUFS], half_src(h)).then_inc(wh_ready, 1)

            def rms_rows(src, name, in_sems, junk):
                at, n = ST[name]
                for t in range(TT):
                    act.wait_ge(in_sems[t], 16)
                    act.activation(junk[:, t, :], src[:, t, :], ACT.Square,
                                   accum_out=stat[:, 0, at + t:at + t + 1]).then_inc(act_seq, 1)
                    n_own[0] += 1
                act.wait_ge(act_seq, n_own[0])
                act.activation(stat[:, 1, at:at + n], stat[:, 0, at:at + n], ACT.Sqrt, bias=lam[:, 6:7],
                               scale=1.0 / D).then_inc(sd_ready, 1)

            def rms_heads(name, dim, count):
                at, n = ST[name]
                act.wait_ge(ss_ready, count)
                act.activation(stat[:, 1, at:at + n], stat[:, 0, at:at + n], ACT.Sqrt, bias=lam[:, 6:7],
                               scale=1.0 / dim).then_inc(sd_ready, 1)

            def hi_of(task, dst, k0, row):
                wait_full(act, task)
                for k in range(4):
                    ins = act.activation(dst[:, k0 + k, :], bank2(misc(task))[:, k, :], ACT.Copy,
                                         scale=vecT[:, row + k0 + k:row + k0 + k + 1])
                ins.then_inc(hi_ready, 1)

            def evac(use, dst, func=ACT.Copy):
                wait_product(act, use)
                act.activation(dst, U[use % 4][:, :].rearrange("p (s n) -> p s n", s=2),
                               func).then_inc(u_free[use % 4], 1)

            def evac_mem(use, dst):
                wait_product(act, use)
                act.wait_ge(mem_rstd_ready, 1)
                at, _n = ST["mem"]
                for t in range(TT):
                    ins = act.activation(dst[:, t, :], U[use % 4][:, 256 * t:256 * t + 256], ACT.Copy,
                                         scale=stat[:, 2, at + t:at + t + 1])
                ins.then_inc(u_free[use % 4], 1)

            def squares(i, name):
                for c in range(2):
                    wait_unit(act, first_unit(name) + c)
                act.activation(cb[:, :, :].rearrange("p a b -> p (a b)"), R[:, i, :], ACT.Square).then_inc(sq_ready, 1)

            def x1_squares(n):
                wait_unit(act, first_unit("out") + n)
                for t in range(TT):
                    act.activation(R[:, 2 + t, 256 * n:256 * n + 256], acc[:, t, 256 * n:256 * n + 256], ACT.Square,
                                   accum_out=x1sq[:, t, n:n + 1]).then_inc(x1sq_ready, 1)

            def squares_y(t):
                wait_read(act, f"dav{t}")
                act.activation(T[:, 1, 512 * t:512 * t + 512], R[:, 3, 512 * t:512 * t + 512],
                               ACT.Square).then_inc(sq_ready, 1)

            def exps(g, task, keys, scale, dst):
                act.wait_ge(nmx_ready, g + 1)
                m = bank2(misc(task))
                for i in range(4):
                    ins = act.activation(dst[:, i, 0:keys], m[:, i, 0:keys], ACT.Exp, scale=scale,
                                         bias=att[:, 1, 4 * g + i:4 * g + i + 1],
                                         accum_out=att[:, 2, 4 * g + i:4 * g + i + 1])
                ins.then_inc(p_ready, 1)

            def to_sbuf(task, dst, cols):
                wait_full(act, task)
                act.copy(dst, misc(task)[:, 0:cols]).then_inc(free_sem(task), 1)

            def hi_y(task, dst, scale):
                wait_full(act, task)
                act.activation(dst, misc(task)[:, 0:512].rearrange("p (h q) -> p h q", h=4), ACT.Copy,
                               scale=scale).then_inc(hi_ready, 1)

            S4 = [S[:, i, :].rearrange("p (m k) -> p m k", m=4) for i in range(2)]

            act.dma_start(PT[V_MEM:V_MEM + 8, 0:P], g_mem.rearrange("a (k p) -> (a k) p", p=P)).then_inc(gmem_in, 16)
            for at, v in ((V_MIX, g_mix), (V_FFN, g_ffn)):
                act.dma_start(PT[at:at + 8, 0:P], v.rearrange("a (k p) -> (a k) p", p=P)).then_inc(vec_in, 16)
            act.wait_ge(eps_ready, 1)
            act.activation(lam[:, 7:8], lam[:, 6:7], ACT.Sqrt)
            split_hi(0)
            wait_read(act, "vecm")
            hi_of("memT0", mTh, 0, V_MEM)
            hi_of("memT1", mTh, 4, V_MEM)
            split_hi(1)
            rms_rows(S, "mem", mem_in, T)
            split_hi(2)
            rms_rows(acc, "x", (x_in, x_in), T)
            for h in range(2, HALVES):
                if 71 <= h <= 73:
                    act.wait_ge(w_used, 70)
                    for i in ((0, 1), (2,), (3,))[h - 71]:
                        act.wait_ge(merged_ready, 9 + i)
                        act.copy(hTh[:, 2 * i:2 * i + 2, :], merged(i)).then_inc(mh_ready, 1)
                if h + 1 < HALVES:
                    split_hi(h + 1)
                if h == 4:
                    wait_read(act, "vec")
                    hi_of("xT0", hTh, 0, V_MIX)
                if h == 5:
                    hi_of("xT1", hTh, 4, V_MIX)
                if h % 2 == 1:
                    c = (h - 3) // 2
                    name, part = units[c]
                    if name in ("mk", "mv"):
                        evac_mem(c, raw(RAW_OF[name])[:, :, 256 * part:256 * part + 256])
                    elif name in RAW_OF:
                        evac(c, raw(RAW_OF[name])[:, :, 256 * part:256 * part + 256])
                    elif name == "cc":
                        evac(c, u[:, 2 * part:2 * part + 2, :])
                    elif name == "cb":
                        evac(c, cb[:, 2 * part:2 * part + 2, :])
                    elif name.startswith("gate"):
                        if c == first_unit("gate2"):
                            wait_full(act, "ds11")
                        used = 4 * merge_order(name) + part - 1
                        if used > 0:
                            act.wait_ge(merged_ready, used)
                        evac(use_of[2 * c], gates(part), ACT.Sigmoid)
                if h == 5:
                    squares(0, "mk")
                if h == 7:
                    rms_heads("mk", 128, 1)
                if h == 13:
                    squares(2, "mq")
                if h == 15:
                    rms_heads("mq", 128, 2)
                if h == 16:
                    act.wait_ge(lam_sum, 1)
                    act.activation(lam[:, 2:4], lam[:, 0:2], ACT.Exp).then_inc(lam_exp, 1)
                if h == 17:
                    squares(3, "dq")
                if h == 19:
                    rms_heads("dq", 64, 3)
                if h == 20:
                    exps(0, "ms0", 256, MEM_SCALE, S4[0])
                if h == 21:
                    exps(1, "ms1", 256, MEM_SCALE, S4[1])
                if h == 23:
                    to_sbuf("mp0", PT[:, :], 1024)
                if h == 24:
                    act.wait_ge(heads_ready, 3)
                    squares(0, "dk")
                if h == 26:
                    rms_heads("dk", 64, 4)
                if h == 25:
                    hi_y("mav0", mTh[:, 0:4, 0:P], 1.0)
                    to_sbuf("mp1", PT[:, :], 1024)
                if h == 27:
                    hi_y("mav1", mTh[:, 0:4, P:2 * P], 1.0)
                if h == 29:
                    to_sbuf("dqT", T[:, 1, :], 1024)
                if h == 31:
                    to_sbuf("dkT", T[:, 0, :], 1024)
                if h == 33:
                    exps(2, "ds00", 128, DIFF_SCALE, S4[0])
                if h == 34:
                    exps(3, "ds01", 128, DIFF_SCALE, S4[1])
                if h == 37:
                    to_sbuf("da0", PT[:, 0:512], 512)
                    exps(4, "ds10", 256, DIFF_SCALE, S4[0])
                if h == 39:
                    to_sbuf("dav0", R[:, 3, 0:512], 512)
                if h == 40:
                    squares_y(0)
                if h == 41:
                    exps(5, "ds11", 256, DIFF_SCALE, S4[1])
                if h == 42:
                    rms_heads("y0", 128, 5)
                if h == 45:
                    to_sbuf("da1", PT[:, :], 1024)
                if h == 47:
                    to_sbuf("dav1", R[:, 3, 512:1024], 512)
                if h == 48:
                    squares_y(1)
                if h == 50:
                    rms_heads("y1", 128, 6)
                if 45 <= h <= 48:
                    k = h - 45
                    act.wait_ge(conv_ready, k + 1)
                    act.copy(ych[:, k, :], S[:, 1, 256 * k:256 * k + 256]).then_inc(ych_ready, 1)
                if h == 49:
                    act.wait_ge(lam_ready, 1)
                    hi_y("dy0", mTh[:, 4:8, 0:P], lam[:, 5:6])
                if h == 54:
                    hi_y("dy1", mTh[:, 4:8, P:2 * P], lam[:, 5:6])
                if h == 74:
                    act.activation(lam[:, 7:8], lam[:, 6:7], ACT.Sqrt)
                    act.wait_ge(cm_in, 16)
                    act.copy(cmb[:, 0, :], cm[:, C_TRI:C_TRI + P])
                    act.copy(cmb[:, 1, :], cm[:, C_ONES:C_ONES + P]).then_inc(cmb_ready, 1)
                if h in (75, 77):
                    act.wait_ge(bgu_in, 16)
                    act.wait_ge(merged_ready, 12)
                    v = slice(D * (h - 75) // 2, D * (h - 75) // 2 + D)
                    act.copy(bguh[:, v], bgu[:, v]).then_inc(bguh_ready, 1)
                if h == 76:
                    x1_squares(0)
                if h == 78:
                    x1_squares(1)

            x1_squares(2)
            x1_squares(3)
            rms_heads("x1", D, 7)
            act.wait_ge(rstd_ready, 1)
            at, _n = ST["x1"]
            for t in range(TT):
                act.activation(X[:, t, :], acc[:, t, :], ACT.Copy,
                               scale=stat[:, 2, at + t:at + t + 1]).then_inc(X_ready, 1)
            act.wait_ge(top_ready, 1)
            for t in range(TT):
                ins = act.activation(gate4[:, t, :], top[:, t, 0:TOP_K], ACT.Exp, bias=gst[:, t, 0:1],
                                     accum_out=gst[:, t, 1:2])
            ins.then_inc(e_ready, 1)
            act.wait_ge(gt_done, 1)
            act.copy(gselT[:, :, :].rearrange("p t n -> p (t n)"), C[0][:, 0:2 * P]).then_inc(gt_ready, 1)
            act.sem_inc(y_ready, 2)

            def pair(n):
                act.wait_ge(gt_done, n + 2)
                act.copy(gselT[:, :, :].rearrange("p t n -> p (t n)"), C[0][:, 0:2 * P]).then_inc(gt_ready, 1)
                for hf in range(2):
                    act.wait_ge(g1_ready, 2 * n + hf + 1)
                    act.activation(sg[:, hf, :], g1[:, hf, :], ACT.Sigmoid, scale=SWIGLU_ALPHA).then_inc(s_ready, 1)
                    act.wait_ge(at_done, 2 * n + hf + 1)
                    act.copy(aT[:, 4 * hf:4 * hf + 4, :].rearrange("p f n -> p (f n)"), C[1 - hf]).then_inc(at_ready, 1)
                act.wait_ge(dn_done, n + 1)
                act.copy(Y[:, 0, :], DN[0]).then_inc(y_ready, 1)

            with act.Fori(0, PAIRS) as p:
                pair(p)
            act.wait_ge(flag_ready, 1)
            more = act.value_load(flag[0:1, 0:1], min_val=0, max_val=1)
            with act.If(more):
                with act.Fori(1, PASSES) as b:
                    with act.Fori(0, PAIRS) as p:
                        pair(b * PAIRS + p)
            act.nop()

        @block.vector
        def _(dve):
            n_own = [0]

            def link(ins):
                n_own[0] += 1
                ins.then_inc(dve_seq, 1)
                dve.wait_ge(dve_seq, n_own[0])

            def split_lo(h):
                dve.wait_ge(wh_ready, h + 1)
                dve.tensor_tensor(WL[:, h % W_BUFS], half_src(h), WH[:, h % W_BUFS].bitcast(F32), ALU.subtract).then_inc(w_ready, 1)

            def inverse(name, order):
                at, n = ST[name]
                dve.wait_ge(sd_ready, order)
                link(dve.reciprocal(stat[:, 2, at:at + n], stat[:, 1, at:at + n]))

            def scale_rows(dst, src, name, signal):
                at, _n = ST[name]
                for t in range(TT):
                    dve.tensor_scalar(dst[:, t, :], src[:, t, :], stat[:, 2, at + t:at + t + 1], None,
                                      ALU.mult).then_inc(signal, 1)

            def lo_of(task, order, dst, hi, k0, row):
                dve.wait_ge(hi_ready, order)
                for k in range(4):
                    ins = dve.scalar_tensor_tensor(
                        out=dst[:, k0 + k, :], in0=bank2(misc(task))[:, k, :],
                        scalar=vecT[:, row + k0 + k:row + k0 + k + 1],
                        in1=hi[:, k0 + k, :].bitcast(F32), op0=ALU.mult, op1=ALU.subtract)
                ins.then_inc(free_sem(task), 1)

            def lo_y(task, order, dst, hi, scale):
                dve.wait_ge(hi_ready, order)
                dve.scalar_tensor_tensor(
                    out=dst, in0=misc(task)[:, 0:512].rearrange("p (h q) -> p h q", h=4), scalar=scale,
                    in1=hi.bitcast(F32), op0=ALU.mult, op1=ALU.subtract).then_inc(free_sem(task), 1)

            def head_sums(name, order, src, dim):
                at, n = ST[name]
                dve.wait_ge(sq_ready, order)
                dve.tensor_reduce(stat[:, 0, at:at + n], src.rearrange("p (g n) -> p g n", n=dim), AX_X,
                                  ALU.add).then_inc(ss_ready, 1)

            def head_norm(name, order, v, dim):
                at, n = ST[name]
                inverse(name, order)
                w = v.rearrange("p (g n) -> p g n", n=dim)
                return dve.tensor_tensor(w, w, stat[:, 2, at:at + n].unsqueeze(2).broadcast_to([P, n, dim]), ALU.mult)

            def gains(i, which):
                w = R[:, i, :].rearrange("p (g n) -> p g n", n=64)
                link(dve.tensor_tensor(w, w, gqk[:, which, :].unsqueeze(1).broadcast_to([P, 16, 64]), ALU.mult))

            def rope(i):
                v = R[:, i, :].rearrange("p (t g n) -> p t g n", t=TT, g=8)
                x1, x2 = v[:, :, :, 0:32], v[:, :, :, 32:64]
                tab = ident[:, P:2 * P].rearrange("p (t c n) -> p t c n", t=TT, c=2)
                cos, sin = (tab[:, :, c, :].unsqueeze(2).broadcast_to([P, TT, 8, 32]) for c in range(2))
                prod = cb[:, :, :].rearrange("p a b -> p (a b)").rearrange("p (c t g n) -> p c t g n", c=2, t=TT, g=8)
                dve.tensor_tensor(prod[:, 0], x1, cos, ALU.mult)
                link(dve.tensor_tensor(prod[:, 1], x1, sin, ALU.mult))
                dve.tensor_tensor(x1, x2, sin, ALU.mult)
                link(dve.tensor_tensor(x2, x2, cos, ALU.mult))
                dve.tensor_tensor(x1, prod[:, 0], x1, ALU.subtract)
                dve.tensor_tensor(x2, x2, prod[:, 1], ALU.add).then_inc(heads_ready, 1)

            def softmax_max(g, task, keys, scale, mask_from=None):
                wait_full(dve, task)
                m = bank2(misc(task))
                if mask_from is not None:
                    link(dve.memset(m[0:64, :, mask_from:mask_from + 64], NEG))
                link(dve.tensor_reduce(att[:, 0, 4 * g:4 * g + 4], m[:, :, 0:keys], AX_X, ALU.max))
                dve.tensor_scalar(att[:, 1, 4 * g:4 * g + 4], att[:, 0, 4 * g:4 * g + 4], -scale, None,
                                  ALU.mult).then_inc(nmx_ready, 1)

            def softmax_norm(g, task, keys, v, diff):
                dve.wait_ge(p_ready, g + 1)
                r = att[:, 3, 4 * g:4 * g + 4]
                link(dve.reciprocal(r, att[:, 2, 4 * g:4 * g + 4]))
                if diff:
                    r2 = r[:, 2:4]
                    link(dve.tensor_scalar(r2, r2, lam[:, 4:5], None, ALU.mult))
                w = v[:, :, 0:keys]
                ins = dve.tensor_tensor(w, w, r.unsqueeze(2).broadcast_to([P, 4, keys]), ALU.mult)
                if diff:
                    link(ins)
                    ins = dve.tensor_tensor(w[:, 0:2, :], w[:, 0:2, :], w[:, 2:4, :], ALU.add)
                ins.then_inc(pn_ready, 1)
                dve.wait_ge(pn_ready, g + 1)
                dve.sem_inc(free_sem(task), 1)

            def conv_chunk(k):
                y = S[:, 1, 256 * k:256 * k + 256]
                w = [vecT[:, V_CONV + 4 * j + k:V_CONV + 4 * j + k + 1] for j in range(3)]
                link(dve.tensor_scalar(y, u[:, k, :], w[2], None, ALU.mult))
                for j in (1, 0):
                    d = 2 - j
                    link(dve.scalar_tensor_tensor(out=y[:, d:256], in0=u[:, k, 0:256 - d], scalar=w[j],
                                                  in1=y[:, d:256], op0=ALU.mult, op1=ALU.add))
                dve.tensor_tensor(y, y, cb[:, k, :], ALU.mult).then_inc(conv_ready, 1)

            def bias_rows(p):
                dve.tensor_tensor(oh[:, :], cm[:, C_EROW:C_EROW + P],
                                  cm[:, bass.ds(C_PM + p, 1)].broadcast_to([P, P]), ALU.is_equal).then_inc(oh_ready, 1)

            def x1_channels(n):
                wait_full(dve, f"XT{n}")
                dve.tensor_tensor(hT2[:, 2 * n:2 * n + 2, :], misc(f"XT{n}")[:, 0:512].rearrange("p (k n) -> p k n", k=2),
                                  vecT[:, V_FFN + 2 * n:V_FFN + 2 * n + 2].unsqueeze(2).broadcast_to([P, 2, SEQ]),
                                  ALU.mult).then_inc(free_sem(f"XT{n}"), 1)

            S4 = [S[:, i, :].rearrange("p (m k) -> p m k", m=4) for i in range(2)]

            dve.memset(lam[:, 6:7], EPS).then_inc(eps_ready, 1)
            wait_full(dve, "vecm")
            dve.tensor_copy(vecT[:, 0:8], misc("vecm")[:, 0:8]).then_inc(free_sem("vecm"), 1)
            split_lo(0)
            wait_read(dve, "vecm")
            lo_of("memT0", 1, mTl, mTh, 0, V_MEM)
            lo_of("memT1", 2, mTl, mTh, 4, V_MEM)
            split_lo(1)
            inverse("mem", 1)
            dve.sem_inc(mem_rstd_ready, 1)
            split_lo(2)
            inverse("x", 2)
            scale_rows(R[:, 2:4, :], acc, "x", xn_ready)
            wait_full(dve, "vec")
            dve.tensor_copy(vecT[:, 8:V_ROWS], misc("vec")[:, 8:V_ROWS]).then_inc(free_sem("vec"), 1)
            wait_read(dve, "vec")
            dve.tensor_scalar(lam[:, 5:6], vecT[:, V_SUB:V_SUB + 1], 1.0 - LAM_INIT, None, ALU.mult).then_inc(lam_ready, 1)

            for h in range(2, HALVES + 2):
                name, part = units[(h - 2) // 2]
                if name.startswith("branch"):
                    use, b, i = use_of[h - 2], merge_order(name), 2 * part + h % 2
                    wait_product(dve, use)
                    wait_unit(dve, first_unit("gate" + name[-1]) + [0, 1, 3, 4][i])
                    if b == 0 and i == 0:
                        wait_full(dve, "mav1")
                    dst = merged(i) if b == 0 else scratch2(i)
                    ins = dve.tensor_tensor(dst, U[use % 4][:, :].rearrange("p (s n) -> p s n", s=2), gates(i), ALU.mult)
                    ins.then_inc(u_free[use % 4], 1)
                    dve.wait_ge(u_free[use % 4], use // 4 + 1)
                    if b == 0:
                        dve.sem_inc(merged_ready, 1)
                    else:
                        dve.tensor_tensor(merged(i), merged(i), scratch2(i), ALU.add).then_inc(merged_ready, 1)
                if 71 <= h <= 73:
                    for i in ((0, 1), (2,), (3,))[h - 71]:
                        dve.wait_ge(mh_ready, i + 1)
                        dve.tensor_tensor(hTl[:, 2 * i:2 * i + 2, :], merged(i), hTh[:, 2 * i:2 * i + 2, :].bitcast(F32),
                                          ALU.subtract).then_inc(ml_ready, 1)
                if h + 1 < HALVES:
                    split_lo(h + 1)
                if h == 4:
                    lo_of("xT0", 3, hTl, hTh, 0, V_MIX)
                if h == 5:
                    lo_of("xT1", 4, hTl, hTh, 4, V_MIX)
                if h % 2 == 1:
                    c = (h - 3) // 2
                    name, part = units[c]
                    if name == "ch":
                        wait_product(dve, c)
                        wait_unit(dve, first_unit("cc") + part)
                        v = u[:, 2 * part:2 * part + 2, :]
                        dve.tensor_tensor(v, U[c % 4][:, :].rearrange("p (s n) -> p s n", s=2), v,
                                          ALU.mult).then_inc(u_free[c % 4], 1)
                    if name == "out":
                        use = use_of[2 * c]
                        wait_product(dve, use)
                        v = acc[:, :, 256 * part:256 * part + 256]
                        dve.tensor_tensor(v, U[use % 4][:, :].rearrange("p (s n) -> p s n", s=2), v,
                                          ALU.add).then_inc(u_free[use % 4], 1)
                cbv = cb[:, :, :].rearrange("p a b -> p (a b)")
                if h == 6:
                    head_sums("mk", 1, cbv, 128)
                if h == 7:
                    head_norm("mk", 3, R[:, 0, :], 128).then_inc(heads_ready, 1)
                if h == 11:
                    wait_full(dve, "mkT")
                    dve.tensor_scalar(T[:, 0, :], misc("mkT")[:, :], vecT[:, V_GKM:V_GKM + 1], None,
                                      ALU.mult).then_inc(free_sem("mkT"), 1)
                if h == 12:
                    dve.wait_ge(lam_in, 64)
                    for i in range(2):
                        ll = PT[:, 256 + 128 * i:384 + 128 * i]
                        ins = dve.tensor_tensor(u[:, i, 0:64], ll[:, 0:64], ll[:, 64:128], ALU.mult)
                    link(ins)
                    dve.tensor_reduce(lam[:, 0:2], u[:, 0:2, 0:64], AX_X, ALU.add).then_inc(lam_sum, 1)
                if h == 14:
                    head_sums("mq", 2, cbv, 128)
                if h == 17:
                    dve.wait_ge(lam_exp, 1)
                    link(dve.scalar_tensor_tensor(out=lam[:, 4:5], in0=lam[:, 3:4], scalar=-LAM_INIT, in1=lam[:, 2:3],
                                                  op0=ALU.add, op1=ALU.subtract))
                if h == 15:
                    head_norm("mq", 4, R[:, 2, :], 128).then_inc(heads_ready, 1)
                if h == 18:
                    wait_full(dve, "mqT")
                    dve.tensor_scalar(T[:, 1, :], misc("mqT")[:, :], vecT[:, V_GQM:V_GQM + 1], None,
                                      ALU.mult).then_inc(free_sem("mqT"), 1)
                    head_sums("dq", 3, cbv, 64)
                if h == 19:
                    softmax_max(0, "ms0", 256, MEM_SCALE)
                    link(head_norm("dq", 5, R[:, 3, :], 64))
                if h == 20:
                    softmax_max(1, "ms1", 256, MEM_SCALE)
                if h == 21:
                    softmax_norm(0, "ms0", 256, S4[0], False)
                if h == 22:
                    softmax_norm(1, "ms1", 256, S4[1], False)
                if h == 23:
                    dve.wait_ge(gqk_in, 32)
                    gains(3, 0)
                if h == 24:
                    rope(3)
                if h == 25:
                    lo_y("mav0", 5, mTl[:, 0:4, 0:P], mTh[:, 0:4, 0:P], 1.0)
                    head_sums("dk", 4, cbv, 64)
                if h == 26:
                    link(head_norm("dk", 6, R[:, 0, :], 64))
                if h == 27:
                    lo_y("mav1", 6, mTl[:, 0:4, P:2 * P], mTh[:, 0:4, P:2 * P], 1.0)
                    gains(0, 1)
                if h == 28:
                    rope(0)
                if h == 33:
                    softmax_max(2, "ds00", 128, DIFF_SCALE, 64)
                    softmax_max(3, "ds01", 128, DIFF_SCALE, 64)
                if h == 34:
                    softmax_norm(2, "ds00", 128, S4[0], True)
                if h == 35:
                    softmax_norm(3, "ds01", 128, S4[1], True)
                if h == 37:
                    softmax_max(4, "ds10", 256, DIFF_SCALE, 192)
                if h == 38:
                    softmax_norm(4, "ds10", 256, S4[0], True)
                if h == 40:
                    softmax_max(5, "ds11", 256, DIFF_SCALE, 192)
                if h == 42:
                    softmax_norm(5, "ds11", 256, S4[1], True)
                if h == 41:
                    head_sums("y0", 5, T[:, 1, 0:512], 128)
                if h == 43:
                    head_norm("y0", 7, R[:, 3, 0:512], 128).then_inc(ydiff_ready, 1)
                if 44 <= h <= 47:
                    if h == 44:
                        wait_full(dve, "da1")
                        for c in range(2):
                            wait_unit(dve, first_unit("cb") + c)
                    conv_chunk(h - 44)
                if 46 <= h <= 49:
                    k = h - 46
                    dve.wait_ge(ych_ready, k + 1)
                    dve.tensor_tensor(ycl[:, k, :], S[:, 1, 256 * k:256 * k + 256], ych[:, k, :].bitcast(F32),
                                      ALU.subtract).then_inc(yconv_ready, 1)
                if h == 49:
                    head_sums("y1", 6, T[:, 1, 512:1024], 128)
                if h == 51:
                    head_norm("y1", 8, R[:, 3, 512:1024], 128).then_inc(ydiff_ready, 1)
                if h == 49:
                    lo_y("dy0", 7, mTl[:, 4:8, 0:P], mTh[:, 4:8, 0:P], lam[:, 5:6])
                if h == 54:
                    lo_y("dy1", 8, mTl[:, 4:8, P:2 * P], mTh[:, 4:8, P:2 * P], lam[:, 5:6])
                if h == 76:
                    dve.memset(gd[:, :, :], 0.0)
                    link(dve.memset(slot[:, :, N_EXPERTS:N_EXPERTS + 2], -1.0))
                if h in (76, 78):
                    v = slice(D * (h - 76) // 2, D * (h - 76) // 2 + D)
                    dve.wait_ge(bguh_ready, (h - 76) // 2 + 1)
                    dve.tensor_tensor(bgul[:, v], bgu[:, v], bguh[:, v].bitcast(F32), ALU.subtract).then_inc(bgul_ready, 1)
                if h in (78, 80, 81):
                    x1_channels({78: 0, 80: 1, 81: 2}[h])
            at, n = ST["x1"]
            dve.wait_ge(x1sq_ready, 4 * TT)
            dve.tensor_reduce(stat[:, 0, at:at + n], x1sq[:, :, :], AX_X, ALU.add).then_inc(ss_ready, 1)
            x1_channels(3)
            inverse("x1", 9)
            dve.sem_inc(rstd_ready, 1)
            dve.wait_ge(wr_in, 32)
            dve.wait_ge(cm_in, 16)
            bias_rows(0)
            dve.wait_ge(logits_done, 1)
            for t in range(TT):
                ins = dve.scalar_tensor_tensor(out=lg[:, t, :], in0=LOGITS[:, t * N_EXPERTS:(t + 1) * N_EXPERTS],
                                               scalar=stat[:, 2, at + t:at + t + 1], in1=br[:, :],
                                               op0=ALU.mult, op1=ALU.add)
            link(ins)
            dve.max(top[:, 0, :], lg[:, 0, :])
            link(dve.max(top[:, 1, :], lg[:, 1, :]))
            dve.tensor_scalar(gst[:, :, 0], top[:, :, 0], -1.0, None, ALU.mult).then_inc(top_ready, 1)
            dve.max_index(topi[:, 0, :], top[:, 0, :], lg[:, 0, :])
            link(dve.max_index(topi[:, 1, :], top[:, 1, :], lg[:, 1, :]))
            link(dve.tensor_copy(topf[:, :, :], topi[:, :, :]))
            every = [P, TT, TOP_K, N_EXPERTS]
            link(dve.tensor_tensor(hot[:, :, 0], cm[:, C_EIOTA:C_EIOTA + N_EXPERTS].unsqueeze(1).unsqueeze(1).broadcast_to(every),
                                   topf[:, :, 0:TOP_K].unsqueeze(3).broadcast_to(every), ALU.is_equal))
            with nc.allow_low_precision(reason="the four indices differ: the sums are 0 or 1"):
                dve.tensor_reduce(msk[:, :, :], hot[:, :, 0].rearrange("p t j e -> p t e j"), AX_X,
                                  ALU.add).then_inc(msk_ready, 1)
            wait_full(dve, "ranks")
            dve.wait_ge(msk_ready, 1)
            m = misc("ranks")
            link(dve.scalar_tensor_tensor(out=slot[:, :, 0:N_EXPERTS], in0=m[:, 0:64].rearrange("p (t e) -> p t e", t=TT),
                                          scalar=1.0, in1=msk[:, :, :], op0=ALU.add, op1=ALU.mult))
            link(dve.tensor_scalar(slot[:, :, 0:N_EXPERTS], slot[:, :, 0:N_EXPERTS], -1.0, None, ALU.add))

            def onehots(p, b, n_gathered):
                if not (isinstance(n_gathered, int) and n_gathered == 0):
                    dve.wait_ge(gather_done, 2 * n_gathered)
                iota = cm[:, bass.ds(C_IOTA + b * SLOT_TOKENS, SLOT_TOKENS)].unsqueeze(1).broadcast_to([P, 2, SLOT_TOKENS])
                for t in range(TT):
                    ins = dve.tensor_tensor(
                        sel[:, t, :].rearrange("p (e s) -> p e s", e=2), iota,
                        slot[:, t, bass.ds(2 * p, 2)].unsqueeze(2).broadcast_to([P, 2, SLOT_TOKENS]), ALU.is_equal)
                ins.then_inc(sel_ready, 1)

            def gathered(k):
                for dh in range(2):
                    dve.wait_ge(gather_done, 2 * k + dh + 1)
                    dve.tensor_tensor(xg[:, 4 * dh:4 * dh + 4, :], DN[dh].rearrange("p (d s) -> p d s", d=4),
                                      vecT[:, V_FFN + 4 * dh:V_FFN + 4 * dh + 4].unsqueeze(2).broadcast_to([P, 4, P]),
                                      ALU.mult).then_inc(xg_ready, 1)

            def add_out(q, k):
                t, hf = q // 2, q % 2
                dve.wait_ge(sc_done, 4 * k + q + 1)
                dve.wait_ge(sc_free, 4 * k + q + 1)
                v = acc[:, t, 512 * hf:512 * hf + 512]
                dve.tensor_tensor(v, MISC[q], v, ALU.add).then_inc(sc_free, 1)

            def swiglu(n, hf, seq):
                if hf == 0:
                    dve.wait_ge(gu_done, n + 1)
                dve.tensor_scalar(g1[:, hf, :], U[hf][:, :], SWIGLU_LIMIT, None, ALU.min).then_inc(g1_ready, 1)
                dve.tensor_scalar(u1[:, hf, :], U[2 + hf][:, :], SWIGLU_LIMIT, -SWIGLU_LIMIT, ALU.min,
                                  ALU.max).then_inc(dve_seq, 1)
                dve.wait_ge(g1_ready, 2 * n + hf + 1)
                dve.wait_ge(dve_seq, seq + 1)
                dve.scalar_tensor_tensor(out=u1[:, hf, :], in0=u1[:, hf, :], scalar=1.0, in1=g1[:, hf, :],
                                         op0=ALU.add, op1=ALU.mult).then_inc(dve_seq, 1)
                dve.wait_ge(dve_seq, seq + 2)
                dve.wait_ge(s_ready, 2 * n + hf + 1)
                dve.tensor_tensor(a[:, 512 * hf:512 * hf + 512], u1[:, hf, :], sg[:, hf, :], ALU.mult).then_inc(a_ready, 1)

            LINKS = 5

            def pair(p, b, n, k, seq):
                onehots(p + 1, b, k + 1)
                iota = cm[:, bass.ds(C_IOTA + b * SLOT_TOKENS, SLOT_TOKENS)].unsqueeze(1).broadcast_to([P, 2, SLOT_TOKENS])
                dve.wait_ge(gt_done, n + 1)
                for t in range(TT):
                    ins = dve.tensor_tensor(
                        gsel[:, t, :].rearrange("p (e s) -> p e s", e=2), iota,
                        slot[:, t, bass.ds(2 * p, 2)].unsqueeze(2).broadcast_to([P, 2, SLOT_TOKENS]), ALU.is_equal)
                ins.then_inc(dve_seq, 1)
                dve.wait_ge(dve_seq, seq + 1)
                for t in range(TT):
                    v = gsel[:, t, :].rearrange("p (e s) -> p e s", e=2)
                    ins = dve.tensor_tensor(
                        v, v, gd[:, t, bass.ds(2 * p, 2)].unsqueeze(2).broadcast_to([P, 2, SLOT_TOKENS]), ALU.mult)
                ins.then_inc(gsel_ready, 1)
                for q in range(4):
                    add_out(q, k)
                swiglu(n, 0, seq + 1)
                dve.wait_ge(chunk_used, n * PAIR_CHUNKS + 16)
                gathered(k + 1)
                swiglu(n, 1, seq + 3)
                bias_rows(p + 1)
                dve.wait_ge(chunk_used, n * PAIR_CHUNKS + PAIR_CHUNKS)
                dve.tensor_copy(Y[:, 1, :], DN[1]).then_inc(y_ready, 1)

            def pairs(b, seq):
                n0, k0 = b * PAIRS, b * (PAIRS + 1)
                with dve.Fori(0, PAIRS) as p:
                    pair(p, b, n0 + p, k0 + p, seq + p * LINKS)
                dve.wait_ge(sc_free, 4 * (k0 + PAIRS) + 4)

            dve.sem_inc(sc_free, 4)
            onehots(0, 0, 0)
            dve.wait_ge(e_ready, 1)
            link(dve.reciprocal(gst[:, :, 2], gst[:, :, 1]))
            link(dve.tensor_tensor(gate4[:, :, :], gate4[:, :, :], gst[:, :, 2:3].broadcast_to([P, TT, TOP_K]), ALU.mult))
            link(dve.tensor_tensor(hot[:, :, 1], hot[:, :, 0], gate4[:, :, :].unsqueeze(3).broadcast_to(every), ALU.mult))
            dve.tensor_reduce(gd[:, :, 0:N_EXPERTS], hot[:, :, 1].rearrange("p t j e -> p t e j"), AX_X,
                              ALU.add).then_inc(gd_ready, 1)
            dve.tensor_reduce(cnt[:, 0:1], m[:, 64:96], AX_X, ALU.max).then_inc(free_sem("ranks"), 1)
            wait_read(dve, "ranks")
            dve.tensor_scalar(flag[0:1, 0:1], cnt[0:1, 0:1], float(SLOT_TOKENS), None, ALU.is_gt).then_inc(flag_ready, 1)
            gathered(0)
            dve.wait_ge(gd_ready, 1)
            dve.wait_ge(flag_ready, 1)
            more = dve.value_load(flag[0:1, 0:1], min_val=0, max_val=1)
            seq0 = n_own[0]
            pairs(0, seq0)
            with dve.If(more):
                with dve.Fori(1, PASSES) as b:
                    k0 = b * (PAIRS + 1)
                    for q in range(4):
                        add_out(q, b * (PAIRS + 1) - 1)
                    dve.memset(Y[:, :, :], 0.0)
                    dve.memset(gselT[:, :, :], 0.0).then_inc(zero_ready, 1)
                    onehots(0, b, k0)
                    bias_rows(0)
                    gathered(k0)
                    pairs(b, seq0 + b * (PAIRS * LINKS))
            for q in range(4):
                t, hf = q // 2, q % 2
                dve.wait_ge(last_done, q + 1)
                v = acc[:, t, 512 * hf:512 * hf + 512]
                dve.tensor_tensor(v, MISC[q], v, ALU.add).then_inc(all_done, 1)


_ORDER = ["x", "mem", "w_in", "w_mem_kv", "w_branch", "w_out", "g_mix", "g_mem", "g_ffn", "conv_w", "g_q_mem", "g_k_mem",
          "g_subln", "g_q_diff", "g_k_diff", "lambda_q1", "lambda_k1", "lambda_q2", "lambda_k2", "w_router", "b_router",
          "w_gate_up", "b_gate_up", "w_down", "b_down"]


def kernel(**inputs):
    import numpy as np
    import concourse.bacc as bacc
    from concourse.bass_utils import run_bass_kernel_spmd

    inv_freq = (1.0 / (np.float32(10000.0) ** (np.arange(0, 64, 2, dtype=np.float32) / np.float32(64)))).astype(np.float32)
    ang = np.arange(SEQ, dtype=np.float32)[:, None] * inv_freq[None, :]
    c_front = np.zeros((P, 256), np.float32)
    c_front[:, :P] = np.eye(P, dtype=np.float32)
    for t in range(TT):
        c_front[:, P + 64 * t:P + 64 * t + 32] = np.cos(ang[t * P:t * P + P])
        c_front[:, P + 64 * t + 32:P + 64 * t + 64] = np.sin(ang[t * P:t * P + P])
    c_moe = np.zeros((P, C_COLS), np.float32)
    row = np.arange(P, dtype=np.float32)
    c_moe[:, C_TRI:C_TRI + P] = row[:, None] < row[None, :]
    c_moe[:, C_IOTA:C_IOTA + SEQ] = np.arange(SEQ)
    c_moe[:, C_EROW:C_EROW + P] = (np.arange(P) // SLOT_TOKENS)[None, :]
    c_moe[:, C_PM:C_PM + PAIRS + 1] = row[:, None] - 2 * np.arange(PAIRS + 1)[None, :]
    c_moe[:, C_EIOTA:C_EIOTA + N_EXPERTS] = np.arange(N_EXPERTS)
    c_moe[:, C_ONES:C_ONES + P] = 1.0

    nc = bacc.Bacc("TRN2", target_bir_lowering=False, num_devices=1)
    arrays, args = {}, []
    for name, v in [(n, inputs[n]) for n in _ORDER] + [("c_front", c_front), ("c_moe", c_moe)]:
        v = np.ascontiguousarray(v)
        arrays[f"in_{name}"] = v
        args.append(nc.dram_tensor(f"in_{name}", v.shape, mybir.dt.from_np(v.dtype), kind="ExternalInput").ap())
    args.append(nc.dram_tensor("out_0", (1, SEQ, D), F32, kind="ExternalOutput").ap())
    build(nc, *args)
    r = run_bass_kernel_spmd(nc, [arrays], core_ids=[0])
    return r.results[0]["out_0"]
```
